# Optimizing a Trainium2 kernel written in Bass

```python
import jax
import jax.numpy as jnp
from jax import lax
import numpy as np

D_MODEL = 1024
BATCH = 1
SEQ = 2048
DEPTH = 1
DEC_BATCH = 8
DEC_SEQ = 4
PAST_LEN = 4096
PAGE_SIZE = 128

HEAD_DIM = 64
W_ATTN = D_MODEL // 2
N_HEADS_A = W_ATTN // HEAD_DIM
W_RG = D_MODEL - W_ATTN
N_RG_BLOCKS = 8
RG_BLOCK = W_RG // N_RG_BLOCKS
CONV_WIDTH = 4
RG_C = 8.0
Q_BLOCK = 128
N_GROUPS = 4
EXPERTS_PER_GROUP = 8
N_EXPERTS = N_GROUPS * EXPERTS_PER_GROUP
TOP_K = 2
D_EXPERT = D_MODEL // 2
EXPERT_BLOCK = 128
RMS_EPS = 1e-6
D_IN = 3 * W_ATTN + 2 * W_RG
SB_BIAS_NEAR = -2.0
SB_BIAS_FAR = -9.0

kernel_name = 'hymba_stickbreak_rglru_hmoe_step'

def rms_norm(x, gain):
    xf = x.astype(jnp.float32)
    y = xf * lax.rsqrt(jnp.mean(xf * xf, axis=-1, keepdims=True) + RMS_EPS)
    return (y * gain.astype(jnp.float32)).astype(x.dtype)

def stick_breaking_block(q, k, v, bias, q_pos, k_pos):
    z = jnp.einsum('bqhd,bkhd->bhqk', q.astype(jnp.float32), k.astype(jnp.float32)) * (HEAD_DIM ** -0.5)
    z = z + bias.astype(jnp.float32)[None, :, None, None]
    causal = k_pos[None, :] < q_pos[:, None]
    log_1m_beta = jnp.where(causal, jax.nn.log_sigmoid(-z), 0.0)
    tail = lax.cumsum(log_1m_beta, axis=3, reverse=True) - log_1m_beta
    w = jnp.where(causal, jnp.exp(jax.nn.log_sigmoid(z) + tail), 0.0)
    return jnp.einsum('bhqk,bkhd->bqhd', w.astype(v.dtype), v)

def stick_breaking_prompt(q, k, v, bias):
    B, T, H, Dh = q.shape
    nb = T // Q_BLOCK
    q_blocks = q.reshape(B, nb, Q_BLOCK, H, Dh).transpose(1, 0, 2, 3, 4)
    q_pos = jnp.arange(T, dtype=jnp.int32).reshape(nb, Q_BLOCK)
    k_pos = jnp.arange(T, dtype=jnp.int32)
    out = lax.map(lambda a: stick_breaking_block(a[0], k, v, bias, a[1], k_pos), (q_blocks, q_pos))
    return out.transpose(1, 0, 2, 3, 4).reshape(B, T, H, Dh)

def causal_conv(xr, buf, w, b):
    T = xr.shape[1]
    xp = jnp.concatenate([buf.astype(xr.dtype), xr], axis=1)
    out = b
    for j in range(CONV_WIDTH):
        out = out + w[j] * xp[:, j:j + T]
    return out, xp[:, T:]

def rg_lru(xc, h0, wa, ba, wx, bx, lam):
    B, T, C = xc.shape
    xf = xc.astype(jnp.float32)
    xh = xf.reshape(B, T, N_RG_BLOCKS, RG_BLOCK)
    r = jax.nn.sigmoid(jnp.einsum('btnc,ncd->btnd', xh, wa.astype(jnp.float32)).reshape(B, T, C) + ba)
    i = jax.nn.sigmoid(jnp.einsum('btnc,ncd->btnd', xh, wx.astype(jnp.float32)).reshape(B, T, C) + bx)
    log_a = -RG_C * r * jax.nn.softplus(-lam.astype(jnp.float32))
    a = jnp.exp(log_a)
    b_in = jnp.sqrt(-jnp.expm1(2.0 * log_a)) * (i * xf)
    b_in = b_in.at[:, 0].add(a[:, 0] * h0.astype(jnp.float32))

    def combine(left, right):
        a1, b1 = left
        a2, b2 = right
        return a1 * a2, a2 * b1 + b2

    _, h = lax.associative_scan(combine, (a, b_in), axis=1)
    return h.astype(xc.dtype), h[:, -1].astype(xc.dtype)

def routed_experts(x, expert_idx, gate, w1, w3, w2):
    n_tok, d = x.shape
    n_slot = expert_idx.shape[0]
    slot_tok = jnp.arange(n_slot, dtype=jnp.int32) // TOP_K
    order = jnp.argsort(expert_idx)
    e_sorted = expert_idx[order]
    counts = jax.ops.segment_sum(jnp.ones_like(expert_idx), expert_idx, num_segments=N_EXPERTS)
    padded = (counts + EXPERT_BLOCK - 1) // EXPERT_BLOCK * EXPERT_BLOCK
    pad_end = jnp.cumsum(padded)
    pad_start = pad_end - padded
    start = jnp.cumsum(counts) - counts
    dest = pad_start[e_sorted] + (jnp.arange(n_slot, dtype=jnp.int32) - start[e_sorted])
    n_blocks = (n_slot + N_EXPERTS * (EXPERT_BLOCK - 1) + EXPERT_BLOCK - 1) // EXPERT_BLOCK
    n_rows = n_blocks * EXPERT_BLOCK
    row_tok = jnp.full((n_rows,), n_tok, jnp.int32).at[dest].set(slot_tok[order])
    row_gate = jnp.zeros((n_rows,), jnp.float32).at[dest].set(gate[order].astype(jnp.float32))
    block_start = jnp.arange(n_blocks, dtype=jnp.int32) * EXPERT_BLOCK
    block_expert = jnp.minimum(jnp.searchsorted(pad_end, block_start, side='right'), N_EXPERTS - 1)
    x_pad = jnp.concatenate([x, jnp.zeros((1, d), x.dtype)], axis=0)

    def expert_block(args):
        toks, e = args
        xb = x_pad[toks]
        hb = jax.nn.silu(xb @ w1[e]) * (xb @ w3[e])
        return hb @ w2[e]

    out = lax.map(expert_block, (row_tok.reshape(n_blocks, EXPERT_BLOCK), block_expert))
    out = out.reshape(n_rows, d) * row_gate[:, None].astype(x.dtype)
    return jax.ops.segment_sum(out, row_tok, num_segments=n_tok + 1)[:n_tok]

def hier_moe(x, w_group, b_group, w_router, b_router, w1, w3, w2):
    n_tok = x.shape[0]
    rows = jnp.arange(n_tok)
    xf = x.astype(jnp.float32)
    g_logits = xf @ w_group.astype(jnp.float32) + b_group.astype(jnp.float32)
    p_group = jax.nn.softmax(g_logits, axis=-1)
    grp = jnp.argmax(g_logits, axis=-1).astype(jnp.int32)
    p_sel = p_group[rows, grp][:, None]
    e_logits = (xf @ w_router.astype(jnp.float32) + b_router.astype(jnp.float32)).reshape(n_tok, N_GROUPS, EXPERTS_PER_GROUP)
    e_in = e_logits[rows, grp]
    top_val, top_idx = lax.top_k(e_in, TOP_K)
    gates = p_sel * jax.nn.softmax(top_val, axis=-1)
    experts = grp[:, None] * EXPERTS_PER_GROUP + top_idx.astype(jnp.int32)
    return routed_experts(x, experts.reshape(-1), gates.reshape(-1), w1, w3, w2)

def decoder_layer(x, c, conv_buf, h0, attend, p):
    B, T, D = x.shape
    mod = (jax.nn.silu(c) @ p['w_ada'] + p['b_ada'])[:, None, :]
    shift1, scale1, gate1, shift2, scale2, gate2 = jnp.split(mod, 6, axis=-1)
    xn = rms_norm(x, p['norm_mix']) * (1 + scale1) + shift1
    proj = xn @ p['w_in']
    q, k, v, xr, yb = jnp.split(proj, [W_ATTN, 2 * W_ATTN, 3 * W_ATTN, 3 * W_ATTN + W_RG], axis=-1)
    q = q.reshape(B, T, N_HEADS_A, HEAD_DIM)
    k = k.reshape(B, T, N_HEADS_A, HEAD_DIM)
    v = v.reshape(B, T, N_HEADS_A, HEAD_DIM)
    attn = rms_norm(attend(q, k, v, p['sb_bias']), p['norm_attn']).reshape(B, T, W_ATTN)
    xc, conv_new = causal_conv(xr, conv_buf, p['conv_w'], p['conv_b'])
    h, h_last = rg_lru(xc, h0, p['rg_wa'], p['rg_ba'], p['rg_wx'], p['rg_bx'], p['rg_lambda'])
    rg = rms_norm(h * jax.nn.gelu(yb), p['norm_rg'])
    x = x + gate1 * (jnp.concatenate([attn, rg], axis=-1) @ p['w_out'])
    xn2 = rms_norm(x, p['norm_ffn']) * (1 + scale2) + shift2
    ffn = hier_moe(xn2.reshape(B * T, D), p['w_group'], p['b_group'], p['w_router'], p['b_router'],
                   p['w1'], p['w3'], p['w2']).reshape(B, T, D)
    x = x + gate2 * ffn
    return x, k, v, conv_new, h_last

def setup_inputs(seed: int = 0) -> dict:
    key = jax.random.key(seed)
    ks = jax.random.split(key, 40)
    n_pages = PAST_LEN // PAGE_SIZE
    n_used = DEC_BATCH * n_pages
    n_phys = n_used + n_used // 4
    f32 = jnp.float32

    def nrm(k, shape, scale=1.0):
        return jax.random.normal(k, shape, f32) * scale

    u = jax.random.uniform(ks[0], (DEPTH, W_RG), f32, minval=0.9, maxval=0.999)
    s = u ** (1.0 / RG_C)
    rg_lambda = jnp.log(s) - jnp.log1p(-s)
    perm = jax.random.permutation(ks[1], n_phys)[:n_used]
    page_table = perm.reshape(DEC_BATCH, n_pages).astype(jnp.int32)
    sb_bias = jnp.linspace(SB_BIAS_NEAR, SB_BIAS_FAR, N_HEADS_A, dtype=f32)[None, :] + nrm(ks[32], (DEPTH, N_HEADS_A), 0.1)
    return {
        'x_prompt': nrm(ks[2], (BATCH, SEQ, D_MODEL)),
        'x_sample': nrm(ks[3], (DEC_BATCH, DEC_SEQ, D_MODEL)),
        'cache_k': nrm(ks[4], (DEPTH, n_phys, PAGE_SIZE, N_HEADS_A, HEAD_DIM)),
        'cache_v': nrm(ks[5], (DEPTH, n_phys, PAGE_SIZE, N_HEADS_A, HEAD_DIM)),
        'state_conv': nrm(ks[6], (DEPTH, DEC_BATCH, CONV_WIDTH - 1, W_RG)),
        'state_h': nrm(ks[7], (DEPTH, DEC_BATCH, W_RG), 0.5),
        'page_table': page_table,
        'c_prompt': nrm(ks[8], (BATCH, D_MODEL)),
        'c_sample': nrm(ks[9], (DEC_BATCH, D_MODEL)),
        'w_ada': nrm(ks[10], (DEPTH, D_MODEL, 6 * D_MODEL), D_MODEL ** -0.5),
        'b_ada': nrm(ks[11], (DEPTH, 6 * D_MODEL), 0.01),
        'norm_mix': 1.0 + nrm(ks[12], (DEPTH, D_MODEL), 0.01),
        'norm_ffn': 1.0 + nrm(ks[13], (DEPTH, D_MODEL), 0.01),
        'w_in': nrm(ks[14], (DEPTH, D_MODEL, D_IN), D_MODEL ** -0.5),
        'sb_bias': sb_bias,
        'norm_attn': 1.0 + nrm(ks[15], (DEPTH, N_HEADS_A, HEAD_DIM), 0.01),
        'conv_w': nrm(ks[16], (DEPTH, CONV_WIDTH, W_RG), CONV_WIDTH ** -0.5),
        'conv_b': nrm(ks[17], (DEPTH, W_RG), 0.01),
        'rg_wa': nrm(ks[18], (DEPTH, N_RG_BLOCKS, RG_BLOCK, RG_BLOCK), RG_BLOCK ** -0.5),
        'rg_ba': nrm(ks[19], (DEPTH, W_RG), 0.01),
        'rg_wx': nrm(ks[20], (DEPTH, N_RG_BLOCKS, RG_BLOCK, RG_BLOCK), RG_BLOCK ** -0.5),
        'rg_bx': nrm(ks[21], (DEPTH, W_RG), 0.01),
        'rg_lambda': rg_lambda,
        'norm_rg': 1.0 + nrm(ks[22], (DEPTH, W_RG), 0.01),
        'w_out': nrm(ks[23], (DEPTH, W_ATTN + W_RG, D_MODEL), (W_ATTN + W_RG) ** -0.5),
        'w_group': nrm(ks[24], (DEPTH, D_MODEL, N_GROUPS), D_MODEL ** -0.5),
        'b_group': nrm(ks[25], (DEPTH, N_GROUPS), 0.01),
        'w_router': nrm(ks[26], (DEPTH, D_MODEL, N_EXPERTS), D_MODEL ** -0.5),
        'b_router': nrm(ks[27], (DEPTH, N_EXPERTS), 0.01),
        'w1': nrm(ks[28], (DEPTH, N_EXPERTS, D_MODEL, D_EXPERT), D_MODEL ** -0.5),
        'w3': nrm(ks[29], (DEPTH, N_EXPERTS, D_MODEL, D_EXPERT), D_MODEL ** -0.5),
        'w2': nrm(ks[30], (DEPTH, N_EXPERTS, D_EXPERT, D_MODEL), D_EXPERT ** -0.5),
        'final_norm': 1.0 + nrm(ks[31], (D_MODEL,), 0.01),
    }

def reference(x_prompt, x_sample, cache_k, cache_v, state_conv, state_h, page_table,
              c_prompt, c_sample, w_ada, b_ada, norm_mix, norm_ffn, w_in, sb_bias, norm_attn,
              conv_w, conv_b, rg_wa, rg_ba, rg_wx, rg_bx, rg_lambda, norm_rg, w_out,
              w_group, b_group, w_router, b_router, w1, w3, w2, final_norm):
    n_seq_s = x_sample.shape[0]
    past_len = page_table.shape[1] * PAGE_SIZE
    xp, xs = x_prompt, x_sample
    kp_all, vp_all, convp_all, hp_all = [], [], [], []
    ks_all, vs_all, convs_all, hs_all = [], [], [], []
    for l in range(DEPTH):
        p = dict(w_ada=w_ada[l], b_ada=b_ada[l], norm_mix=norm_mix[l], norm_ffn=norm_ffn[l],
                 w_in=w_in[l], sb_bias=sb_bias[l], norm_attn=norm_attn[l], conv_w=conv_w[l],
                 conv_b=conv_b[l], rg_wa=rg_wa[l], rg_ba=rg_ba[l], rg_wx=rg_wx[l], rg_bx=rg_bx[l],
                 rg_lambda=rg_lambda[l], norm_rg=norm_rg[l], w_out=w_out[l],
                 w_group=w_group[l], b_group=b_group[l], w_router=w_router[l],
                 b_router=b_router[l], w1=w1[l], w3=w3[l], w2=w2[l])

        def attend_sample(q, k, v, bias, l=l):
            t_new = q.shape[1]
            k_past = cache_k[l][page_table].reshape(n_seq_s, past_len, N_HEADS_A, HEAD_DIM)
            v_past = cache_v[l][page_table].reshape(n_seq_s, past_len, N_HEADS_A, HEAD_DIM)
            keys = jnp.concatenate([k_past, k.astype(k_past.dtype)], axis=1)
            vals = jnp.concatenate([v_past, v.astype(v_past.dtype)], axis=1)
            q_pos = past_len + jnp.arange(t_new, dtype=jnp.int32)
            k_pos = jnp.arange(past_len + t_new, dtype=jnp.int32)
            return stick_breaking_block(q, keys, vals, bias, q_pos, k_pos)

        conv0 = jnp.zeros((xp.shape[0], CONV_WIDTH - 1, W_RG), xp.dtype)
        h0 = jnp.zeros((xp.shape[0], W_RG), jnp.float32)
        xp, kp, vp, convp, hp = decoder_layer(xp, c_prompt, conv0, h0, stick_breaking_prompt, p)
        xs, k_s, v_s, convs, hs = decoder_layer(xs, c_sample, state_conv[l], state_h[l], attend_sample, p)
        kp_all.append(kp)
        vp_all.append(vp)
        convp_all.append(convp)
        hp_all.append(hp)
        ks_all.append(k_s)
        vs_all.append(v_s)
        convs_all.append(convs)
        hs_all.append(hs)
    y_prompt = rms_norm(xp, final_norm)
    y_sample = rms_norm(xs, final_norm)
    k_prompt = jnp.stack(kp_all)
    v_prompt = jnp.stack(vp_all)
    conv_prompt = jnp.stack(convp_all)
    h_prompt = jnp.stack(hp_all)
    k_sample = jnp.stack(ks_all)
    v_sample = jnp.stack(vs_all)
    conv_sample = jnp.stack(convs_all)
    h_sample = jnp.stack(hs_all)
    return (y_prompt, y_sample, k_prompt, v_prompt, conv_prompt, h_prompt, k_sample, v_sample, conv_sample, h_sample)


_drawn_inputs = setup_inputs


def setup_inputs(seed=0):
    import zlib

    import numpy as np

    out = dict(_drawn_inputs(seed))
    spreads = {}
    factors = {'norm_mix': 3.584,
     'norm_ffn': 3.688,
     'norm_attn': 8.0,
     'conv_b': 3.585,
     'rg_ba': 8.0,
     'rg_bx': 7.692,
     'norm_rg': 3.674,
     'b_group': 4.635,
     'b_router': 5.473,
     'final_norm': 5.736}
    for name, (base, spread) in spreads.items():
        noise = np.random.default_rng([zlib.crc32(name.encode()), seed]).standard_normal(out[name].shape)
        drawn = base * np.exp(spread * noise) if base else spread * noise
        out[name] = jnp.asarray(drawn.astype(out[name].dtype))
    for name, factor in factors.items():
        out[name] = (out[name] * factor).astype(out[name].dtype)
    return out
```

```python
import math
from contextlib import ExitStack

import numpy as np
import concourse.bass as bass
from concourse import mybir

F32 = mybir.dt.float32
BF16 = mybir.dt.bfloat16
I32 = mybir.dt.int32
U32 = mybir.dt.uint32
ALU = mybir.AluOpType
ACT = mybir.ActivationFunctionType
AX_X = mybir.AxisListType.X

P = 128
D = 1024
KC = D // P
SEQ = 2048
BS, TS = 8, 4
NS = BS * TS
NTOK = SEQ + NS
PAST, PAGE = 4096, 128
NPAGES = PAST // PAGE
NPHYS = 320
H, DH = 8, 64
WA = H * DH
WR = D - WA
FC = WR // P
CONV = 4
RGC = 8.0
NG, EPG = 4, 8
NE = NG * EPG
DE = D // 2
EC = DE // P
CAP = SEQ + P
FILL = 136
MAX_BLOCKS = 2 * NTOK // P + 1 + NE
NO_ROW = 1 << 20
EPS = 1e-6
GRP = 512
NGRP = SEQ // GRP
TPG = GRP // P
NT = SEQ // P
SCALE = float(DH) ** -0.5
GELU_IN = 0.044715
GELU_OUT = 2.0 * math.sqrt(2.0 / math.pi)

VEC_ROWS, _n = {}, 0
for _name, _rows in (("b_ada", 48), ("norm_mix", KC), ("conv_w", CONV * FC), ("conv_b", FC), ("rg_ba", FC),
                     ("rg_bx", FC), ("rg_lambda", FC), ("norm_rg", FC), ("norm_attn", FC)):
    VEC_ROWS[_name] = (_n, _rows)
    _n += _rows
NVEC = _n
SHIFT1, SCALE1, GATE1, SHIFT2, SCALE2, GATE2 = (KC * i for i in range(6))


def ds(start, size):
    return bass.ds(start, size)


class Kit:

    def __init__(self, nc, stack, clears=True):
        self.nc, self.stack, self.sems = nc, stack, []
        if clears:
            stack.callback(self.clear)

    def sb(self, name, shape, dt=F32):
        return self.stack.enter_context(self.nc.sbuf_tensor(name, shape, dt))

    def ps(self, name, shape, dt=F32):
        return self.stack.enter_context(self.nc.psum_tensor(name, shape, dt))

    def sem(self, name):
        self.sems.append(self.nc.alloc_semaphore(name=name))
        return self.sems[-1]

    def clear(self):
        if self.sems:
            self.nc.clear_and_free_semaphores(self.sems)
            self.nc.all_engine_barrier()


def hold(eng, sem, value, passed):
    eng.wait_ge(sem, value)
    eng.sem_inc(passed, 1)


def modulation_phase(nc, io, keep, sems):
    BUFS = 4
    with ExitStack() as stack:
        k = Kit(nc, stack)
        vec_rows = k.sb("vec_rows", [NVEC, P])
        c_rows = k.sb("c_rows", [1 + BS, D])
        c_sig = k.sb("c_sig", [1 + BS, D])
        cT = k.sb("cT", [P, KC, 1 + BS])
        wada = [k.sb(f"wada{i}", [P, KC, 512]) for i in range(BUFS)]
        conv_rows = k.sb("conv_rows", [BS * (CONV - 1), WR])
        h_rows = k.sb("h_rows", [BS, WR])
        lam = [k.sb(f"lam{i}", [P, FC]) for i in range(6)]
        ps_t = k.ps("ps_t", [P, 512])
        ps_c = k.ps("ps_c", [P, 512])
        ps_s = k.ps("ps_s", [P, 512])
        ps_m = [k.ps(f"ps_m{i}", [P, 512]) for i in range(2)]
        s_vec, s_c, s_st, s_small, s_bias = (k.sem(f"p1_{n}") for n in ("vec", "c", "st", "small", "bias"))
        s_wada = [k.sem(f"p1_wada{i}") for i in range(BUFS)]
        s_id, s_csig, s_cs, s_pt, s_ct, s_mm, s_ev, s_el = (
            k.sem(f"p1_{n}") for n in ("id", "csig", "cs", "pt", "ct", "mm", "ev", "el"))
        ident, ones = keep["ident"], keep["ones"]
        vecT, modT = keep["vecT"], keep["modT"]
        w_ada = io["w_ada"][0].rearrange("(c p) n -> p c n", p=P)
        NCH = 6 * D // 512
        with nc.Block() as block:

            @block.sync
            def _(sp):
                for name, (row, rows) in VEC_ROWS.items():
                    src = io[name][0]
                    if name in ("conv_w", "norm_attn"):
                        src = src.rearrange("j n -> (j n)")
                    sp.dma_start(vec_rows[row:row + rows, :], src.rearrange("(a p) -> a p", p=P)).then_inc(s_vec, 16)
                sp.dma_start(c_rows[0:1, :], io["c_prompt"]).then_inc(s_c, 16)
                sp.dma_start(c_rows[1:1 + BS, :], io["c_sample"]).then_inc(s_c, 16)
                sp.dma_start(conv_rows[:, :], io["state_conv"][0].rearrange("b j n -> (b j) n")).then_inc(s_st, 16)
                sp.dma_start(h_rows[:, :], io["state_h"][0]).then_inc(s_st, 16)
                sp.dma_start(keep["biasP"][:, :], io["sb_bias"][0].rearrange("(a n) -> a n", a=1).to_broadcast([P, H])).then_inc(s_bias, 16)
                with sp.Fori(0, NCH // BUFS) as i:
                    for b in range(BUFS):
                        sp.wait_ge(s_ev, BUFS * i + b + 1)
                        sp.dma_start(wada[b][:, :, :], w_ada[:, :, ds((BUFS * i + b) * 512, 512)]).then_inc(s_wada[b], 16)
                sp.dma_start(keep["w_in"][:, :, :], io["w_in"][0].rearrange("(c p) n -> p c n", p=P)).then_inc(sems["w_in"], 16)
                sp.wait_ge(s_id, 3)
                for n, name in enumerate(("rg_wa", "rg_wx")):
                    w = io[name][0].rearrange("(f two) c d -> two c f d", two=2)
                    for half in range(2):
                        at = slice(64 * half, 64 * half + 64)
                        sp.dma_start(keep["w_gate"][at, n, :, at], w[half]).then_inc(s_small, 16)
                sp.wait_ge(s_small, 64)

            @block.gpsimd
            def _(pool):
                pool.memset(ident[:, :], 0.0)
                pool.memset(keep["eps"][:, :], EPS)
                pool.memset(ones[:, :], 1.0).then_inc(s_id, 1)
                pool.drain()
                pool.affine_select(out=ident[:, :], in_=ident[:, :], compare_op=ALU.not_equal, fill=1.0,
                                   base=0, pattern=[[-1, P]], channel_multiplier=1).then_inc(s_id, 1)
                pool.memset(keep["w_gate"][:, :, :, :], 0.0).then_inc(s_id, 1)
                pool.nop().then_inc(s_ev, BUFS)

            @block.scalar
            def _(act):
                act.wait_ge(s_c, 32)
                act.activation(c_sig[:, :], c_rows[:, :], ACT.Sigmoid).then_inc(s_csig, 1)
                act.wait_ge(s_el, 1)
                act.activation(lam[1][:, :], lam[0][:, :], ACT.Exp).then_inc(s_el, 1)

            @block.tensor
            def _(pe):
                pe.wait_ge(s_id, 3)
                pe.wait_ge(s_vec, 16 * len(VEC_ROWS))
                pe.transpose(ps_t[:, 0:NVEC], vec_rows[:, :], ident[0:NVEC, 0:NVEC]).then_inc(s_pt, 1)
                pe.wait_ge(s_cs, 1)
                for c in range(KC):
                    mm = pe.transpose(ps_c[:, 9 * c:9 * c + 9], c_rows[:, c * P:c * P + P], ident[0:9, 0:9])
                mm.then_inc(s_pt, 1)
                pe.wait_ge(s_st, 32)
                for f in range(FC):
                    pe.transpose(ps_s[:, 24 * f:24 * f + 24], conv_rows[:, f * P:f * P + P], ident[0:24, 0:24])
                    mm = pe.transpose(ps_s[:, 96 + 8 * f:104 + 8 * f], h_rows[:, f * P:f * P + P], ident[0:8, 0:8])
                mm.then_inc(s_pt, 1)
                pe.wait_ge(s_ct, 1)
                with pe.Fori(0, NCH // BUFS) as i:
                    for b in range(BUFS):
                        pe.wait_ge(s_wada[b], 16 * i + 16)
                        pe.wait_ge(s_ev, BUFS * i + b + BUFS - 1)
                        for ft in range(4):
                            for c in range(KC):
                                mm = pe.matmul(ps_m[b % 2][:, 9 * ft:9 * ft + 9], wada[b][:, c, ft * P:ft * P + P],
                                               cT[:, c, :], start=(c == 0), stop=(c == KC - 1))
                        mm.then_inc(s_mm, 1)

            @block.vector
            def _(dve):
                dve.wait_ge(s_csig, 1)
                dve.tensor_tensor(c_rows[:, :], c_rows[:, :], c_sig[:, :], ALU.mult).then_inc(s_cs, 1)
                dve.wait_ge(s_pt, 1)
                dve.tensor_copy(vecT[:, :], ps_t[:, 0:NVEC])
                dve.wait_ge(s_pt, 2)
                dve.tensor_copy(cT[:, :, :], ps_c[:, 0:KC * 9].rearrange("p (c n) -> p c n", c=KC)).then_inc(s_ct, 1)
                dve.wait_ge(s_pt, 3)
                dve.tensor_copy(keep["conv0"][:, :, :], ps_s[:, 0:96].rearrange("p (f n) -> p f n", f=FC))
                dve.tensor_copy(keep["h0"][:, :, :], ps_s[:, 96:128].rearrange("p (f n) -> p f n", f=FC))
                dve.drain()
                l0 = vecT[:, VEC_ROWS["rg_lambda"][0]:VEC_ROWS["rg_lambda"][0] + FC]
                dve.tensor_scalar(lam[2][:, :], l0, -1.0, None, ALU.mult)
                dve.drain()
                dve.tensor_tensor(lam[0][:, :], l0, lam[2][:, :], ALU.min).then_inc(s_el, 1)
                dve.wait_ge(s_bias, 16)
                dve.wait_ge(s_el, 2)
                dve.tensor_scalar(lam[3][:, :], lam[1][:, :], 2.0, None, ALU.add)
                dve.drain()
                dve.reciprocal(lam[3][:, :], lam[3][:, :])
                dve.drain()
                dve.tensor_tensor(lam[3][:, :], lam[3][:, :], lam[1][:, :], ALU.mult)
                dve.drain()
                dve.tensor_tensor(lam[4][:, :], lam[3][:, :], lam[3][:, :], ALU.mult)
                dve.memset(lam[5][:, :], 1.0 / 17)
                for n in (15, 13, 11, 9, 7, 5, 3, 1):
                    dve.drain()
                    dve.tensor_tensor(lam[5][:, :], lam[5][:, :], lam[4][:, :], ALU.mult)
                    dve.drain()
                    dve.tensor_scalar(lam[5][:, :], lam[5][:, :], 1.0 / n, None, ALU.add)
                dve.drain()
                dve.tensor_tensor(lam[5][:, :], lam[5][:, :], lam[3][:, :], ALU.mult)
                dve.tensor_scalar(lam[2][:, :], lam[2][:, :], 0.0, None, ALU.max)
                dve.drain()
                dve.scalar_tensor_tensor(out=lam[5][:, :], in0=lam[5][:, :], scalar=2.0, in1=lam[2][:, :],
                                         op0=ALU.mult, op1=ALU.add)
                dve.drain()
                dve.tensor_scalar(keep["coef"][:, :], lam[5][:, :], -RGC, None, ALU.mult)
                with dve.Fori(0, NCH // BUFS) as i:
                    for b in range(BUFS):
                        dve.wait_ge(s_mm, BUFS * i + b + 1)
                        at = (BUFS * i + b) * 4
                        dve.tensor_tensor(modT[:, ds(at, 4), :], ps_m[b % 2][:, 0:36].rearrange("p (f n) -> p f n", f=4),
                                          vecT[:, ds(at, 4)].unsqueeze(2).to_broadcast([P, 4, 9]), ALU.add).then_inc(s_ev, 1)
                dve.drain()
                r = VEC_ROWS["norm_mix"][0]
                dve.scalar_tensor_tensor(out=keep["A1T"][:, :, :], in0=modT[:, SCALE1:SCALE1 + KC, :], scalar=1.0,
                                         in1=vecT[:, r:r + KC].unsqueeze(2).to_broadcast([P, KC, 9]), op0=ALU.add, op1=ALU.mult)
                dve.tensor_scalar(keep["nbiasP"][:, :], keep["biasP"][:, :], -1.0, None, ALU.mult)
                dve.drain()
JOBS = ([(f"xT{c}", "dve") for c in range(KC)] + [(f"xr{f}", "act") for f in range(FC)] +
        [(f"yb{f}", "act") for f in range(FC)] + [(f"q{f}", "dve") for f in range(FC)] +
        [(f"r{f}", "act") for f in range(FC)] + [(f"i{f}", "act") for f in range(FC)] +
        [(f"v{j}", "act") for j in range(TPG)] + [(f"k{j}", "dve") for j in range(TPG)] +
        [(f"kT{f}", "dve") for f in range(FC)] + [("rms", "act")])
JOB = {name: n for n, (name, _) in enumerate(JOBS)}
NJ = len(JOBS)


def emptied(n, engine):
    return sum(e == engine for _, e in JOBS[:n + 1])


def projection_phase(nc, io, keep, sems):
    with ExitStack() as stack:
        k = Kit(nc, stack)
        x_t = k.sb("x_t", [P, TPG, D])
        ssq = k.sb("ssq", [P, TPG])
        rstd = k.sb("rstd", [P, TPG])
        xnT = k.sb("xnT", [P, KC, GRP])
        xr = k.sb("xr", [P, FC, CONV - 1 + GRP])
        xc = k.sb("xc", [P, FC, GRP])
        ra = k.sb("ra", [P, FC, GRP])
        ig = k.sb("ig", [P, FC, GRP])
        yb = k.sb("yb", [P, FC, GRP])
        gt = k.sb("gt", [P, FC, GRP])
        th = k.sb("th", [P, FC, GRP])
        hs = th
        h_last = k.sb("h_last", [P, FC])
        qk_st = k.sb("qk_st", [P, FC, GRP])
        v_st = k.sb("v_st", [P, TPG, WA])
        k_st = k.sb("k_st", [P, TPG, WA])
        rrow = k.sb("rrow", [P, GRP])
        junk = rrow[:, :].bitcast(BF16)
        bank = [k.ps(f"bank{i}", [P, 512]) for i in range(8)]
        made, act_out, dve_out = k.sem("p2_made"), k.sem("p2_act_out"), k.sem("p2_dve_out")
        s_x, s_xn, s_rs, s_sq, s_sp = (k.sem(f"p2_{n}") for n in ("x", "xn", "rs", "sq", "sp"))
        s_xc, s_ga, s_th, s_m2, s_m, s_sig, s_gp, s_gy, s_rg, s_rq, s_rt, s_rgn = (
            k.sem(f"p2_{n}") for n in ("xc", "ga", "th", "m2", "m", "sig", "gp", "gy", "rg", "rq", "rt", "rgn"))
        st_q, st_v, st_k, st_kT, st_rg, s_tail, s_stored = (
            k.sem(f"p2_st_{n}") for n in ("q", "v", "k", "kT", "rg", "tail", "all"))
        ident, ones, vecT, modT, w_in = (keep[n] for n in ("ident", "ones", "vecT", "modT", "w_in"))
        wcol = {"q": 0, "k": WA, "v": 2 * WA, "xr": 3 * WA, "yb": 3 * WA + WR}
        n_of = {e: emptied(NJ - 1, e) for e in ("act", "dve")}
        out_sem = {"act": act_out, "dve": dve_out}

        def vcol(name, n):
            r = VEC_ROWS[name][0] + n
            return vecT[:, r:r + 1]

        def wait_out(eng, name, g):
            n = JOB[name]
            e = JOBS[n][1]
            eng.wait_ge(out_sem[e], (g + 1) * n_of[e] + emptied(n, e))

        def out_value(name, g):
            n = JOB[name]
            return (g + 1) * n_of[JOBS[n][1]] + emptied(n, JOBS[n][1])

        def wait_made(eng, name, g):
            eng.wait_ge(made, g * NJ + JOB[name] + 1)

        x_d = io["x_prompt"][0].rearrange("(g j p) n -> g p j n", j=TPG, p=P)
        rows = lambda name: io[name][0, 0].rearrange("(g j p) h d -> g p j (h d)", j=TPG, p=P)
        cols = lambda ap: ap.rearrange("(f p) (g t) -> g p f t", p=P, t=GRP)
        qT_d, kT_d, rgT_d = cols(io["qT_d"]), cols(io["kT_d"]), cols(io["rgT_d"])
        v_d, k_d = rows("v_prompt"), rows("k_prompt")

        with nc.Block() as block:

            @block.sync
            def _(sp):
                sp.nop().then_inc(s_stored, 1)
                sp.dma_start(x_t[:, :, :], x_d[0]).then_inc(s_x, 16)
                with sp.Fori(0, NGRP) as g:
                    nxt = sp.snap((g + 1) & (NGRP - 1))
                    at = {n: sp.snap(out_value(n, g)) for n in (f"q{FC - 1}", f"v{TPG - 1}", f"k{TPG - 1}", f"kT{FC - 1}")}
                    turned = sp.snap(g * NJ + JOB[f"xT{KC - 1}"] + 1)
                    one_more, stored = sp.snap(g + 1), sp.snap(16 * g + 16)
                    hold(sp, made, turned, s_sp)
                    sp.dma_start(x_t[:, :, :], x_d[ds(nxt, 1)].rearrange("a p j n -> (a p) j n")).then_inc(s_x, 16)

                    def store(dst, src, sem, name=None):
                        if name:
                            hold(sp, out_sem[JOBS[JOB[name]][1]], at[name], s_sp)
                        sp.dma_start(dst[ds(g, 1)].rearrange("a p j n -> (a p) j n"), src).then_inc(sem, 16)

                    store(qT_d, qk_st[:, :, :], st_q, f"q{FC - 1}")
                    store(v_d, v_st[:, :, :], st_v, f"v{TPG - 1}")
                    store(k_d, k_st[:, :, :], st_k, f"k{TPG - 1}")
                    store(kT_d, qk_st[:, :, :], st_kT, f"kT{FC - 1}")
                    hold(sp, s_rgn, one_more, s_sp)
                    store(rgT_d, hs[:, :, :], st_rg)
                    for s in (st_v, st_k, st_kT, st_rg):
                        hold(sp, s, stored, s_sp)
                    sp.nop().then_inc(s_stored, 1)
                with nc.allow_non_contiguous_dma(reason="a few thousand bytes"):
                    conv_o = io["conv_prompt"][0, 0].rearrange("j (f p) -> f p j", p=P)
                    for f in range(FC):
                        sp.dma_start(conv_o[f], xr[:, f, 0:CONV - 1]).then_inc(s_tail, 16)
                    sp.dma_start(io["h_prompt"][0].rearrange("a (f p) -> p (a f)", p=P), h_last[:, :]).then_inc(s_tail, 16)
                for s, n in ((st_q, NGRP), (st_v, NGRP), (st_k, NGRP), (st_kT, NGRP), (st_rg, NGRP), (s_tail, FC + 1), (s_x, NGRP + 1)):
                    sp.wait_ge(s, 16 * n)

            @block.tensor
            def _(pe):
                with pe.Fori(0, NGRP) as g:

                    def free_bank(n):
                        before = [m for m in range(NJ) if m % 8 == n % 8]
                        at = before.index(n)
                        m = before[at - 1]
                        e = JOBS[m][1]
                        pe.wait_ge(out_sem[e], (g + (1 if at else 0)) * n_of[e] + emptied(m, e))
                        return bank[n % 8]

                    pe.wait_ge(s_xn, g + 1)
                    for c in range(KC):
                        ps = free_bank(JOB[f"xT{c}"])
                        for j in range(TPG):
                            mm = pe.transpose(ps[:, j * P:j * P + P], x_t[:, j, c * P:c * P + P], ident[:, :])
                        mm.then_inc(made, 1)

                    def product(name, parts):
                        ps = free_bank(JOB[name])
                        for i, (w, m) in enumerate(parts):
                            mm = pe.matmul(ps[:, :], w, m, start=(i == 0), stop=(i == len(parts) - 1))
                        mm.then_inc(made, 1)

                    for c in range(KC):
                        wait_out(pe, f"xT{c}", g)
                    pe.wait_ge(sems["w_in"], 16)
                    for part in ("xr", "yb", "q"):
                        for f in range(FC):
                            at = wcol[part] + f * P
                            product(f"{part}{f}", [(w_in[:, c, at:at + P], xnT[:, c, :]) for c in range(KC)])
                    pe.wait_ge(s_xc, g + 1)
                    for n, part in enumerate(("r", "i")):
                        for f in range(FC):
                            product(f"{part}{f}", [(keep["w_gate"][:, n, f, :], xc[:, f, :])])
                    for part in ("v", "k"):
                        at = wcol[part]
                        for j in range(TPG):
                            product(f"{part}{j}", [(xnT[:, c, j * P:j * P + P], w_in[:, c, at:at + WA]) for c in range(KC)])
                    wait_out(pe, f"k{TPG - 1}", g)
                    for f in range(FC):
                        ps = free_bank(JOB[f"kT{f}"])
                        for j in range(TPG):
                            mm = pe.transpose(ps[:, j * P:j * P + P], k_st[:, j, f * P:f * P + P], ident[:, :])
                        mm.then_inc(made, 1)
                    pe.wait_ge(s_rq, g + 1)
                    product("rms", [(ones[:, :], gt[:, f, :]) for f in range(FC)])

            @block.scalar
            def _(act):
                act.nop().then_inc(act_out, n_of["act"])

                def norm(n):
                    act.wait_ge(s_x, n * 16)
                    for j in range(TPG):
                        if j:
                            act.drain()
                        act.activation(junk, x_t[:, j, :], ACT.Square, scale=1.0 / math.sqrt(D),
                                       accum_out=ssq[:, j:j + 1])
                    act.drain()
                    act.activation(ssq[:, :], ssq[:, :], ACT.Sqrt, bias=keep["eps"][:, 0:1]).then_inc(s_sq, 1)
                    act.wait_ge(s_rs, n)
                    for j in range(TPG):
                        last = act.activation(x_t[:, j, :], x_t[:, j, :], ACT.Copy, scale=rstd[:, j:j + 1])
                    last.then_inc(s_xn, 1)

                norm(1)
                with act.Fori(0, NGRP) as g:
                    for f in range(FC):
                        wait_made(act, f"xr{f}", g)
                        act.activation(xr[:, f, CONV - 1:], bank[JOB[f"xr{f}"] % 8][:, :], ACT.Copy).then_inc(act_out, 1)
                    for f in range(FC):
                        wait_made(act, f"yb{f}", g)
                        act.activation(yb[:, f, :], bank[JOB[f"yb{f}"] % 8][:, :], ACT.Copy).then_inc(act_out, 1)
                    act.wait_ge(s_gp, g + 1)
                    act.activation(gt[:, :, :], gt[:, :, :], ACT.Sigmoid, scale=GELU_OUT).then_inc(s_sig, 1)
                    for f in range(FC):
                        wait_made(act, f"r{f}", g)
                        act.activation(ra[:, f, :], bank[JOB[f"r{f}"] % 8][:, :], ACT.Sigmoid, bias=vcol("rg_ba", f)).then_inc(act_out, 1)
                    for f in range(FC):
                        wait_made(act, f"i{f}", g)
                        act.activation(ig[:, f, :], bank[JOB[f"i{f}"] % 8][:, :], ACT.Sigmoid, bias=vcol("rg_bx", f)).then_inc(act_out, 1)
                    hold(act, s_stored, g + 1, s_sp)
                    act.drain()
                    for f in range(FC):
                        act.activation(th[:, f, :], ra[:, f, :], ACT.Tanh, scale=keep["coef"][:, f:f + 1])
                    act.drain()
                    for f in range(FC):
                        last = act.activation(ra[:, f, :], ra[:, f, :], ACT.Exp, scale=keep["coef"][:, f:f + 1])
                    act.drain().then_inc(s_th, 1)

                    def values(first, last):
                        for j in range(first, last):
                            wait_made(act, f"v{j}", g)
                            act.activation(v_st[:, j, :], bank[JOB[f"v{j}"] % 8][:, :], ACT.Copy).then_inc(act_out, 1)

                    values(0, 2)
                    norm(g + 2)
                    values(2, TPG)
                    act.wait_ge(s_m2, g + 1)
                    act.activation(th[:, :, :], th[:, :, :], ACT.Sqrt, scale=-1.0).then_inc(s_m, 1)
                    act.wait_ge(s_rg, g + 1)
                    act.activation(gt[:, :, :], hs[:, :, :], ACT.Square, scale=1.0 / math.sqrt(WR)).then_inc(s_rq, 1)
                    wait_made(act, "rms", g)
                    act.activation(rrow[:, :], bank[JOB["rms"] % 8][:, :], ACT.Sqrt, bias=keep["eps"][:, 0:1]).then_inc(act_out, 1)

            @block.vector
            def _(dve):
                dve.nop().then_inc(dve_out, n_of["dve"])
                dve.memset(xr[:, :, 0:CONV - 1], 0.0)
                dve.memset(h_last[:, :], 0.0)

                def inverse(n):
                    dve.wait_ge(s_sq, n)
                    dve.reciprocal(rstd[:, :], ssq[:, :]).then_inc(s_rs, 1)

                inverse(1)
                with dve.Fori(0, NGRP) as g:
                    for c in range(KC):
                        wait_made(dve, f"xT{c}", g)
                        dve.tensor_scalar(xnT[:, c, :], bank[JOB[f"xT{c}"] % 8][:, :], keep["A1T"][:, c, 0:1],
                                          modT[:, SHIFT1 + c, 0:1], ALU.mult, ALU.add).then_inc(dve_out, 1)
                    for tap in range(CONV):
                        dve.drain()
                        for f in range(FC):
                            w = vcol("conv_w", tap * FC + f)
                            if tap == 0:
                                wait_out(dve, f"xr{f}", g)
                                dve.tensor_scalar(xc[:, f, :], xr[:, f, 0:GRP], w, vcol("conv_b", f), ALU.mult, ALU.add)
                            else:
                                dve.scalar_tensor_tensor(out=xc[:, f, :], in0=xr[:, f, tap:tap + GRP], scalar=w,
                                                         in1=xc[:, f, :], op0=ALU.mult, op1=ALU.add)
                    dve.drain().then_inc(s_xc, 1)
                    dve.tensor_copy(xr[:, :, 0:CONV - 1], xr[:, :, GRP:GRP + CONV - 1])
                    dve.wait_ge(s_stored, g + 1)
                    for f in range(FC):
                        wait_made(dve, f"q{f}", g)
                        dve.tensor_copy(qk_st[:, f, :], bank[JOB[f"q{f}"] % 8][:, :]).then_inc(dve_out, 1)
                    dve.wait_ge(s_th, g + 1)
                    dve.tensor_tensor(ig[:, :, :], ig[:, :, :], xc[:, :, :], ALU.mult)
                    dve.drain()
                    dve.tensor_tensor(xc[:, :, :], ra[:, :, :], ra[:, :, :], ALU.mult)
                    dve.drain()
                    dve.scalar_tensor_tensor(out=th[:, :, :], in0=xc[:, :, :], scalar=1.0, in1=th[:, :, :],
                                             op0=ALU.add, op1=ALU.mult).then_inc(s_m2, 1)
                    inverse(g + 2)
                    dve.wait_ge(s_m, g + 1)
                    dve.tensor_tensor(ig[:, :, :], ig[:, :, :], th[:, :, :], ALU.mult)
                    dve.drain()
                    for f in range(FC):
                        dve.tensor_tensor_scan(hs[:, f, :], ra[:, f, :], ig[:, f, :], h_last[:, f:f + 1], ALU.mult, ALU.add)
                    dve.drain()
                    dve.tensor_copy(h_last[:, :], hs[:, :, GRP - 1])
                    dve.drain()
                    dve.wait_ge(s_gy, g + 1)
                    dve.tensor_tensor(hs[:, :, :], hs[:, :, :], yb[:, :, :], ALU.mult).then_inc(s_rg, 1)
                    for j in range(TPG):
                        wait_made(dve, f"k{j}", g)
                        dve.tensor_copy(k_st[:, j, :], bank[JOB[f"k{j}"] % 8][:, :]).then_inc(dve_out, 1)
                    dve.wait_ge(st_q, 16 * g + 16)
                    for f in range(FC):
                        wait_made(dve, f"kT{f}", g)
                        dve.tensor_copy(qk_st[:, f, :], bank[JOB[f"kT{f}"] % 8][:, :]).then_inc(dve_out, 1)
                    wait_out(dve, "rms", g)
                    dve.reciprocal(rrow[:, :], rrow[:, :])
                    dve.drain()
                    for f in range(FC):
                        dve.scalar_tensor_tensor(out=hs[:, f, :], in0=hs[:, f, :], scalar=vcol("norm_rg", f),
                                                 in1=rrow[:, :], op0=ALU.mult, op1=ALU.mult)
                    dve.drain().then_inc(s_rgn, 1)

            @block.gpsimd
            def _(pool):
                with pool.Fori(0, NGRP) as g:
                    wait_out(pool, f"yb{FC - 1}", g)
                    pool.tensor_tensor(gt[:, :, :], yb[:, :, :], yb[:, :, :], ALU.mult)
                    pool.drain()
                    pool.tensor_scalar(gt[:, :, :], gt[:, :, :], GELU_IN, 1.0, ALU.mult, ALU.add)
                    pool.drain()
                    pool.tensor_tensor(gt[:, :, :], gt[:, :, :], yb[:, :, :], ALU.mult).then_inc(s_gp, 1)
                    pool.wait_ge(s_sig, g + 1)
                    pool.tensor_tensor(yb[:, :, :], yb[:, :, :], gt[:, :, :], ALU.mult).then_inc(s_gy, 1)


def sample_projection_phase(nc, io, keep, sems):
    with ExitStack() as stack:
        k = Kit(nc, stack)
        x_s = k.sb("x_s", [NS, D])
        junk = k.sb("junk_s", [NS, D], BF16)
        ssq = k.sb("ssq_s", [NS, 2])
        xnT = k.sb("xnT_s", [P, KC, NS])
        ext = k.sb("ext_s", [P, FC, BS, CONV - 1 + TS])
        xc, ra, ig, yb, gt, th, hs = (k.sb(f"{n}_s", [P, FC, NS]) for n in ("xc", "ra", "ig", "yb", "gt", "th", "hs"))
        tmp = k.sb("tmp_s", [P, FC, BS])
        vT = k.sb("vT_s", [P, FC, NS])
        conv_l = k.sb("conv_l", [P, FC, BS * (CONV - 1)])
        h_l = k.sb("h_l", [P, FC, BS])
        k_row, v_row = k.sb("k_row", [NS, WA]), k.sb("v_row", [NS, WA])
        conv_row, h_row = k.sb("conv_row", [BS * (CONV - 1), WR]), k.sb("h_row", [BS, WR])
        rrow = k.sb("rrow_s", [P, NS])
        ps = {n: k.ps(f"ps3_{n}", [P, 512]) for n in ("a", "b", "xr", "yb", "q", "k", "v", "g")}
        s = {n: k.sem(f"p3_{n}") for n in ("x", "sq", "rs", "xn", "xT", "xnT", "proj", "ext", "yb", "kv", "kvT", "row", "xc",
                                            "gate", "ri", "th", "m2", "m", "gp", "sig", "h", "last", "lastT", "rg", "rq", "rms",
                                            "rt", "lrow", "st")}
        ident, ones, vecT, modT, w_in = (keep[n] for n in ("ident", "ones", "vecT", "modT", "w_in"))
        wcol = {"q": 0, "k": WA, "v": 2 * WA, "xr": 3 * WA, "yb": 3 * WA + WR}
        seqs = lambda t: t[:, :, :].rearrange("p f (b t) -> p f b t", b=BS)

        def vcol(name, n):
            r = VEC_ROWS[name][0] + n
            return vecT[:, r:r + 1]

        with nc.Block() as block:

            @block.sync
            def _(sp):
                sp.dma_start(x_s[:, :], io["x_sample"].rearrange("b t n -> (b t) n")).then_inc(s["x"], 16)
                sp.wait_ge(s["row"], 2)
                sp.dma_start(io["k_sample"][0].rearrange("b t h d -> (b t) (h d)"), k_row[:, :]).then_inc(s["st"], 16)
                sp.dma_start(io["v_sample"][0].rearrange("b t h d -> (b t) (h d)"), v_row[:, :]).then_inc(s["st"], 16)
                sp.wait_ge(s["lrow"], 2)
                sp.dma_start(io["conv_sample"][0].rearrange("b j n -> (b j) n"), conv_row[:, :]).then_inc(s["st"], 16)
                sp.dma_start(io["h_sample"][0], h_row[:, :]).then_inc(s["st"], 16)
                sp.wait_ge(s["st"], 64)

            @block.scalar
            def _(act):
                act.wait_ge(s["x"], 16)
                act.activation(junk[:, :], x_s[:, :], ACT.Square, scale=1.0 / math.sqrt(D), accum_out=ssq[:, 0:1])
                act.drain()
                act.activation(ssq[:, 0:1], ssq[:, 0:1], ACT.Sqrt, bias=keep["eps"][0:NS, 0:1]).then_inc(s["sq"], 1)
                act.wait_ge(s["rs"], 1)
                act.activation(x_s[:, :], x_s[:, :], ACT.Copy, scale=ssq[:, 1:2]).then_inc(s["xn"], 1)
                act.wait_ge(s["proj"], 5)
                act.activation(yb[:, :, :], ps["yb"][:, 0:FC * NS].rearrange("p (f n) -> p f n", f=FC), ACT.Copy).then_inc(s["yb"], 1)
                act.wait_ge(s["gp"], 1)
                act.activation(gt[:, :, :], gt[:, :, :], ACT.Sigmoid, scale=GELU_OUT).then_inc(s["sig"], 1)
                act.wait_ge(s["gate"], 1)
                for f in range(FC):
                    act.activation(ra[:, f, :], ps["g"][:, f * NS:f * NS + NS], ACT.Sigmoid, bias=vcol("rg_ba", f))
                    at = (FC + f) * NS
                    act.activation(ig[:, f, :], ps["g"][:, at:at + NS], ACT.Sigmoid, bias=vcol("rg_bx", f))
                act.drain()
                for f in range(FC):
                    act.activation(th[:, f, :], ra[:, f, :], ACT.Tanh, scale=keep["coef"][:, f:f + 1])
                act.drain()
                for f in range(FC):
                    act.activation(ra[:, f, :], ra[:, f, :], ACT.Exp, scale=keep["coef"][:, f:f + 1])
                act.drain().then_inc(s["th"], 1)
                act.wait_ge(s["m2"], 1)
                act.activation(th[:, :, :], th[:, :, :], ACT.Sqrt, scale=-1.0).then_inc(s["m"], 1)
                act.wait_ge(s["rg"], 1)
                act.activation(gt[:, :, :], hs[:, :, :], ACT.Square, scale=1.0 / math.sqrt(WR)).then_inc(s["rq"], 1)
                act.wait_ge(s["rms"], 1)
                act.activation(rrow[:, :], ps["b"][:, 0:NS], ACT.Sqrt, bias=keep["eps"][:, 0:1]).then_inc(s["rt"], 1)

            @block.tensor
            def _(pe):
                pe.wait_ge(s["xn"], 1)
                for c in range(KC):
                    mm = pe.transpose(ps["a"][:, c * NS:c * NS + NS], x_s[:, c * P:c * P + P], ident[0:NS, 0:NS])
                mm.then_inc(s["xT"], 1)
                pe.wait_ge(s["xnT"], 1)
                for part in ("xr", "yb", "q", "k", "v"):
                    for f in range(FC):
                        at = wcol[part] + f * P
                        for c in range(KC):
                            mm = pe.matmul(ps[part][:, f * NS:f * NS + NS], w_in[:, c, at:at + P], xnT[:, c, :],
                                           start=(c == 0), stop=(c == KC - 1))
                    mm.then_inc(s["proj"], 1)
                pe.wait_ge(s["kv"], 2)
                for part, src in (("a", keep["kT_new"]), ("b", vT)):
                    for f in range(FC):
                        mm = pe.transpose(ps[part][0:NS, f * P:f * P + P], src[:, f, :], ident[:, :])
                    mm.then_inc(s["kvT"], 1)
                pe.wait_ge(s["xc"], 1)
                for n in range(2):
                    for f in range(FC):
                        at = (n * FC + f) * NS
                        mm = pe.matmul(ps["g"][:, at:at + NS], keep["w_gate"][:, n, f, :], xc[:, f, :], start=True, stop=True)
                mm.then_inc(s["gate"], 1)
                pe.wait_ge(s["last"], 1)
                pe.wait_ge(s["row"], 2)
                for f in range(FC):
                    pe.transpose(ps["xr"][0:BS * (CONV - 1), f * P:f * P + P], conv_l[:, f, :], ident[:, :])
                    mm = pe.transpose(ps["q"][0:BS, f * P:f * P + P], h_l[:, f, :], ident[:, :])
                mm.then_inc(s["lastT"], 1)
                pe.wait_ge(s["rq"], 1)
                for f in range(FC):
                    mm = pe.matmul(ps["b"][:, 0:NS], ones[:, :], gt[:, f, :], start=(f == 0), stop=(f == FC - 1))
                mm.then_inc(s["rms"], 1)

            @block.vector
            def _(dve):
                dve.wait_ge(s["sq"], 1)
                dve.reciprocal(ssq[:, 1:2], ssq[:, 0:1]).then_inc(s["rs"], 1)
                dve.tensor_copy(ext[:, :, :, 0:CONV - 1], keep["conv0"][:, :, :].rearrange("p f (b j) -> p f b j", b=BS))
                dve.wait_ge(s["xT"], 1)
                x4 = xnT[:, :, :].rearrange("p c (b t) -> p c b t", b=BS)
                dve.tensor_tensor(x4, ps["a"][:, 0:KC * NS].rearrange("p (c b t) -> p c b t", c=KC, b=BS),
                                  keep["A1T"][:, :, 1:].unsqueeze(3).to_broadcast([P, KC, BS, TS]), ALU.mult)
                dve.drain()
                dve.tensor_tensor(x4, x4, modT[:, SHIFT1:SHIFT1 + KC, 1:].unsqueeze(3).to_broadcast([P, KC, BS, TS]),
                                  ALU.add).then_inc(s["xnT"], 1)
                bank4 = lambda n: ps[n][:, 0:FC * NS].rearrange("p (f b t) -> p f b t", f=FC, b=BS)
                dve.wait_ge(s["proj"], 5)
                dve.tensor_copy(ext[:, :, :, CONV - 1:], bank4("xr"))
                dve.tensor_copy(seqs(keep["kT_new"]), bank4("k")).then_inc(s["kv"], 1)
                dve.tensor_copy(seqs(vT), bank4("v")).then_inc(s["kv"], 1)
                dve.memset(keep["q_blk"][:, :, :, :], 0.0)
                dve.drain()
                for pair in range(H // 2):
                    for half in range(2):
                        rows = slice(64 * half, 64 * half + 64)
                        c0 = (2 * pair + half) * TS
                        dve.tensor_copy(keep["q_blk"][rows, :, pair, c0:c0 + TS],
                                        ps["q"][rows, pair * NS:pair * NS + NS].rearrange("p (b t) -> p b t", b=BS))
                for tap in range(CONV):
                    dve.drain()
                    for f in range(FC):
                        w = vcol("conv_w", tap * FC + f)
                        out = xc[:, f, :].rearrange("p (b t) -> p b t", b=BS)
                        if tap == 0:
                            dve.tensor_scalar(out, ext[:, f, :, 0:TS], w, vcol("conv_b", f), ALU.mult, ALU.add)
                        else:
                            dve.scalar_tensor_tensor(out=out, in0=ext[:, f, :, tap:tap + TS], scalar=w, in1=out,
                                                     op0=ALU.mult, op1=ALU.add)
                dve.drain().then_inc(s["xc"], 1)
                dve.wait_ge(s["kvT"], 2)
                dve.tensor_copy(k_row[:, :], ps["a"][0:NS, :]).then_inc(s["row"], 1)
                dve.tensor_copy(v_row[:, :], ps["b"][0:NS, :]).then_inc(s["row"], 1)
                dve.wait_ge(s["yb"], 1)
                dve.tensor_tensor(gt[:, :, :], yb[:, :, :], yb[:, :, :], ALU.mult)
                dve.drain()
                dve.tensor_scalar(gt[:, :, :], gt[:, :, :], GELU_IN, 1.0, ALU.mult, ALU.add)
                dve.drain()
                dve.tensor_tensor(gt[:, :, :], gt[:, :, :], yb[:, :, :], ALU.mult).then_inc(s["gp"], 1)
                dve.wait_ge(s["sig"], 1)
                dve.tensor_tensor(yb[:, :, :], yb[:, :, :], gt[:, :, :], ALU.mult)
                dve.wait_ge(s["th"], 1)
                dve.tensor_tensor(ig[:, :, :], ig[:, :, :], xc[:, :, :], ALU.mult)
                dve.drain()
                dve.tensor_tensor(xc[:, :, :], ra[:, :, :], ra[:, :, :], ALU.mult)
                dve.drain()
                dve.scalar_tensor_tensor(out=th[:, :, :], in0=xc[:, :, :], scalar=1.0, in1=th[:, :, :],
                                         op0=ALU.add, op1=ALU.mult).then_inc(s["m2"], 1)
                dve.wait_ge(s["m"], 1)
                dve.tensor_tensor(ig[:, :, :], ig[:, :, :], th[:, :, :], ALU.mult)
                dve.drain()
                a4, b4, h4 = seqs(ra), seqs(ig), seqs(hs)
                for t in range(TS):
                    before = keep["h0"][:, :, :] if t == 0 else h4[:, :, :, t - 1]
                    dve.tensor_tensor(tmp[:, :, :], a4[:, :, :, t], before, ALU.mult)
                    dve.drain()
                    dve.tensor_tensor(h4[:, :, :, t], tmp[:, :, :], b4[:, :, :, t], ALU.add)
                    dve.drain()
                dve.tensor_copy(h_l[:, :, :], h4[:, :, :, TS - 1])
                dve.tensor_copy(conv_l[:, :, :].rearrange("p f (b j) -> p f b j", b=BS), ext[:, :, :, TS:]).then_inc(s["last"], 1)
                dve.drain()
                dve.tensor_tensor(hs[:, :, :], hs[:, :, :], yb[:, :, :], ALU.mult).then_inc(s["rg"], 1)
                dve.wait_ge(s["lastT"], 1)
                dve.tensor_copy(conv_row[:, :], ps["xr"][0:BS * (CONV - 1), :]).then_inc(s["lrow"], 1)
                dve.tensor_copy(h_row[:, :], ps["q"][0:BS, :]).then_inc(s["lrow"], 1)
                dve.wait_ge(s["rt"], 1)
                dve.reciprocal(rrow[:, :], rrow[:, :])
                dve.drain()
                for f in range(FC):
                    dve.scalar_tensor_tensor(out=keep["rgT_new"][:, f, :], in0=hs[:, f, :], scalar=vcol("norm_rg", f),
                                             in1=rrow[:, :], op0=ALU.mult, op1=ALU.mult)
                dve.drain()


def prompt_attention_phase(nc, io, keep):
    AHEAD = 3
    with ExitStack() as stack:
        k = Kit(nc, stack)
        kT = k.sb("kT", [P, FC, SEQ])
        vv = k.sb("vv", [P, NT, WA])
        mask = k.sb("mask", [P, TPG, GRP], BF16)
        identb = k.sb("identb", [P, P], BF16)
        q_pad = [k.sb(f"q_pad{i}", [P, P]) for i in range(4)]
        take = [k.sb(f"take{i}", [P, GRP]) for i in range(4)]
        leave = [k.sb(f"leave{i}", [P, GRP]) for i in range(4)]
        left = [k.sb(f"left{i}", [P, SEQ + 1]) for i in range(2)]
        w = [k.sb(f"w{i}", [P, GRP]) for i in range(4)]
        wT = [k.sb(f"wT{i}", [P, TPG, P]) for i in range(2)]
        zb = [k.ps(f"zb{i}", [P, GRP]) for i in range(4)]
        tb = [k.ps(f"tb{i}", [P, GRP]) for i in range(2)]
        ob = [k.ps(f"ob{i}", [P, 512]) for i in range(2)]
        s_kv, s_zero, s_set, s_z, s_sg, s_scan, s_w, s_t, s_wT, s_pv, s_o, s_sp, s_act = (
            k.sem(f"p4_{n}") for n in ("kv", "zero", "set", "z", "sg", "scan", "w", "t", "wT", "pv", "o", "sp", "act"))
        s_q = [k.sem(f"p4_q{i}") for i in range(4)]
        ident, o_nat = keep["ident"], keep["o_nat"]
        ROUNDS = 8
        steps = lambda g: 4 * (g + 1)
        base = lambda g: sum(ROUNDS * steps(i) for i in range(g))
        tbase = lambda g: base(g) + 2 * g
        q_src = io["qT_d"].rearrange("(p hh d) (t q) -> hh p t d q", hh=2, d=DH, q=P)

        def pair_of(x):
            return (x >> 1) & (H // 2 - 1)

        def item_of(g, s):
            i, c = s // (g + 1), g - s % (g + 1)
            return i, i // 2, i % 2, c

        with nc.Block() as block:

            @block.sync
            def _(sp):
                sp.dma_start(kT[:, :, :], io["kT_d"].rearrange("(f p) t -> p f t", p=P)).then_inc(s_kv, 16)
                sp.dma_start(vv[:, :, :], io["v_prompt"][0, 0].rearrange("(t p) h d -> p t (h d)", p=P)).then_inc(s_kv, 16)
                sp.wait_ge(s_zero, 4)

                def load_q(g, x, i):
                    r2, par = i // 2, i % 2
                    pair, tile = pair_of(x), 4 * g + 2 * (x & 1) + r2
                    sp.dma_start(q_pad[i][64 * par:64 * par + 64, :],
                                 q_src[par, ds(pair, 1), ds(tile, 1)].rearrange("a b d q -> (a b d) q")).then_inc(s_q[i], 16)

                for i in range(4):
                    load_q(0, 0, i)
                for g in range(NGRP):
                    S = steps(g)
                    with sp.Fori(0, ROUNDS - 1) as x:
                        used = [sp.snap(base(g) + x * S + (i + 1) * (g + 1)) for i in range(4)]
                        nxt = sp.snap(x + 1)
                        for i in range(4):
                            hold(sp, s_z, used[i], s_sp)
                            load_q(g, nxt, i)
                    if g + 1 < NGRP:
                        for i in range(4):
                            sp.wait_ge(s_z, base(g) + (ROUNDS - 1) * S + (i + 1) * (g + 1))
                            load_q(g + 1, 0, i)

            @block.gpsimd
            def _(pool):
                pool.memset(mask[:, :, :], 0.0)
                pool.memset(identb[:, :], 0.0)
                pool.drain()
                pool.affine_select(out=mask[:, :, :], in_=mask[:, :, :], compare_op=ALU.is_gt, fill=-1.0e30, base=0,
                                   pattern=[[P, TPG], [-1, GRP]], channel_multiplier=1)
                pool.affine_select(out=identb[:, :], in_=identb[:, :], compare_op=ALU.not_equal, fill=1.0, base=0,
                                   pattern=[[-1, P]], channel_multiplier=1)
                pool.drain().then_inc(s_set, 1)
                pool.nop().then_inc(s_w, 4)
                for g in range(NGRP):
                    S = steps(g)
                    with pool.Fori(0, ROUNDS) as x:
                        for s in range(S):
                            i, r2, par, c = item_of(g, s)
                            n = x * S + s
                            pool.wait_ge(s_scan, base(g) + n + 1)
                            pool.wait_ge(s_t, tbase(g) + n + 1)
                            pool.tensor_tensor(w[s % 4][:, :], take[s % 4][:, :],
                                               left[i % 2][:, c * GRP + 1:(c + 1) * GRP + 1], ALU.mult).then_inc(s_w, 1)

            @block.scalar
            def _(act):
                act.nop().then_inc(s_sg, 4)
                for g in range(NGRP):
                    S = steps(g)
                    with act.Fori(0, ROUNDS) as x:
                        for s in range(S):
                            i, r2, par, c = item_of(g, s)
                            n = x * S + s
                            head = 2 * pair_of(x) + par
                            act.wait_ge(s_z, base(g) + n + 1)
                            hold(act, s_w, base(g) + n + 1, s_act)
                            act.activation(leave[s % 4][:, :], zb[s % 4][:, :], ACT.Sigmoid, scale=-SCALE,
                                           bias=keep["nbiasP"][:, ds(head, 1)])
                            act.activation(take[s % 4][:, :], zb[s % 4][:, :], ACT.Sigmoid, scale=SCALE,
                                           bias=keep["biasP"][:, ds(head, 1)]).then_inc(s_sg, 1)

            @block.vector
            def _(dve):
                for i in range(4):
                    dve.memset(q_pad[i][64 * (1 - i % 2):64 * (1 - i % 2) + 64, :], 0.0).then_inc(s_zero, 1)
                for i in range(2):
                    dve.memset(ob[i][:, :], 0.0)
                    dve.memset(tb[i][:, :], 0.0)
                dve.drain()

                def unturn(g, n, s):
                    dve.wait_ge(s_t, 2 + tbase(g) + n + 1)
                    dve.wait_ge(s_pv, base(g) + n + 1)
                    dve.tensor_copy(wT[s % 2][:, :, :], tb[s % 2][:, :].rearrange("p (j q) -> p j q", j=TPG)).then_inc(s_wT, 1)

                def outputs(g, x, r2, made):
                    dve.wait_ge(s_pv, made)
                    prev = (x + ROUNDS - 1) & (ROUNDS - 1)
                    at = (4 * g + 2 * (prev & 1) + r2) * WA + pair_of(prev) * P
                    dve.tensor_copy(o_nat[:, :, :].rearrange("p t n -> p (t n)")[:, ds(at, P)], ob[r2][:, 0:P]).then_inc(s_o, 1)

                for g in range(NGRP):
                    S = steps(g)
                    for i in range(2):
                        dve.memset(left[i][:, (g + 1) * GRP:(g + 1) * GRP + 1], 1.0)
                    dve.drain()
                    with dve.Fori(0, ROUNDS) as x:
                        for s in range(S):
                            i, r2, par, c = item_of(g, s)
                            n = x * S + s
                            dve.wait_ge(s_sg, 4 + base(g) + n + 1)
                            if c == g:
                                dve.wait_ge(s_w, base(g) + n - g + (4 if g else 3))
                            at, end = c * GRP, (c + 1) * GRP
                            dve.tensor_tensor_scan(left[i % 2][:, at:end][:, ::-1], leave[s % 4][:, ::-1], leave[s % 4][:, ::-1],
                                                   left[i % 2][:, end:end + 1], ALU.mult, ALU.bypass).then_inc(s_scan, 1)
                            unturn(g, n, s)
                            if s in (1, 3):
                                r = s // 2
                                outputs(g, x, r, 4 + base(g) + x * S - (2 * (g + 1) if r == 0 else 0))
                            dve.drain()
                    for s in range(2):
                        unturn(g, ROUNDS * S + s, s)
                    for r in range(2):
                        outputs(g, ROUNDS, r, 4 + base(g) + ROUNDS * S - (2 * (g + 1) if r == 0 else 0))
                    dve.drain()

            @block.tensor
            def _(pe):
                pe.wait_ge(s_kv, 32)
                pe.wait_ge(s_set, 1)
                pe.wait_ge(s_zero, 4)
                pe.nop().then_inc(s_pv, 4)
                pe.nop().then_inc(s_t, 2)

                def scores(g, x, s):
                    i, r2, par, c = item_of(g, s)
                    n = x * steps(g) + s
                    if c == g:
                        pe.wait_ge(s_q[i], 16 * (ROUNDS * g + x) + 16)
                    pe.wait_ge(s_sg, base(g) + n + 1)
                    pair = pair_of(x)
                    keys = kT[:, :, :].rearrange("p f t -> p (f t)")[:, ds(pair * SEQ + c * GRP, GRP)]
                    mm = pe.matmul(zb[s % 4][:, :], q_pad[i][:, :], keys, start=True, stop=(c != g))
                    if c == g:
                        r = 2 * (x & 1) + r2
                        mm = pe.matmul(zb[s % 4][:, :], identb[:, :], mask[:, :, :].rearrange("p r s -> p (r s)")[:, ds(r * GRP, GRP)],
                                       start=False, stop=True)
                    mm.then_inc(s_z, 1)

                def turn(g, x, s):
                    n = x * steps(g) + s
                    pe.wait_ge(s_w, 4 + base(g) + n + 1)
                    pe.wait_ge(s_wT, tbase(g) + n + 1)
                    for j in range(TPG):
                        mm = pe.transpose(tb[s % 2][:, j * P:j * P + P], w[s % 4][:, j * P:j * P + P], ident[:, :])
                    mm.then_inc(s_t, 1)

                def values(g, x, s):
                    i, r2, par, c = item_of(g, s)
                    n = x * steps(g) + s
                    if c == g and par == 0:
                        pe.wait_ge(s_o, 18 * g + 2 * x + r2 + 1)
                    pe.wait_ge(s_wT, 2 + tbase(g) + n + 1)
                    col = (2 * pair_of(x) + par) * DH
                    for j in range(TPG):
                        rhs = vv[:, :, :].rearrange("p t n -> p (t n)")[:, ds((c * TPG + j) * WA + col, DH)]
                        mm = pe.matmul(ob[r2][:, par * DH:par * DH + DH], wT[s % 2][:, j, :], rhs,
                                       start=(c == g and j == 0), stop=(c == 0 and j == TPG - 1))
                    mm.then_inc(s_pv, 1)

                def a_round(g, x, last):
                    S = steps(g)
                    for s in range(S):
                        if s + AHEAD < S:
                            scores(g, x, s + AHEAD)
                        elif not last:
                            scores(g, x + 1, s + AHEAD - S)
                        turn(g, x, s)
                        if s:
                            values(g, x, s - 1)
                    values(g, x, S - 1)

                for g in range(NGRP):
                    for s in range(AHEAD):
                        scores(g, 0, s)
                    pe.drain().then_inc(s_t, 2)
                    with pe.Fori(0, ROUNDS - 1) as x:
                        a_round(g, x, False)
                    a_round(g, ROUNDS - 1, True)


def sample_attention_phase(nc, io, keep):
    PPC = 4
    CH = PPC * PAGE
    NY = PAST // CH
    NU = 2 * NY
    with ExitStack() as stack:
        k = Kit(nc, stack)
        pages = k.sb("pages", [1, BS * NPAGES], I32)
        kp = [k.sb(f"kp{j}", [P, PPC, WA]) for j in range(4)]
        vp = [k.sb(f"vp{j}", [P, PPC, WA]) for j in range(4)]
        kTs = [k.sb(f"kTs{j}", [P, FC, CH]) for j in range(2)]
        take, leave, w = (k.sb(f"s_{n}", [P, CH]) for n in ("take", "leave", "w"))
        left = k.sb("s_left", [P, CH + 1])
        take_n, leave_n, w_n = (k.sb(f"n_{n}", [P, TS]) for n in ("take", "leave", "w"))
        left_n = k.sb("n_left", [P, TS + 1])
        wT = k.sb("s_wT", [P, PPC, P])
        wT_n = k.sb("n_wT", [TS, P])
        v_new = k.sb("v_new", [TS, BS, WA])
        bias, nbias = k.sb("s_bias", [P, 1]), k.sb("s_nbias", [P, 1])
        gain = k.sb("s_gain", [P, DH])
        tok, low = k.sb("tok", [TS, P], BF16), k.sb("low", [TS, TS], BF16)
        band = k.sb("band", [P, 4, H])
        own = k.sb("own", [P, H])
        o_all = k.sb("o_all", [P, H, DH])
        o_row, o_sq = k.sb("o_row", [P, DH]), k.sb("o_sq", [P, DH])
        ssq = k.sb("s_ssq", [P, 2])
        kb = [k.ps(f"kb{i}", [P, CH]) for i in range(4)]
        zb, wb, ob = k.ps("s_zb", [P, CH]), k.ps("s_wb", [P, CH]), k.ps("s_ob", [P, WA])
        s_pg, s_small, s_set, s_nb, s_kt, s_kd, s_ka, s_z, s_sg, s_scan, s_w, s_tw, s_wt, s_pv, s_o, s_sp, s_os, s_rs, s_on, s_oT = (
            k.sem(f"p5_{n}") for n in ("pg", "small", "set", "nb", "kt", "kd", "ka", "z", "sg", "scan", "w", "tw", "wt", "pv", "o",
                                      "sp", "os", "rs", "on", "oT"))
        s_k = [k.sem(f"p5_k{j}") for j in range(4)]
        s_v = [k.sem(f"p5_v{j}") for j in range(4)]
        ident = keep["ident"]
        cache = {"k": io["cache_k"][0].rearrange("n p h d -> n p (h d)"), "v": io["cache_v"][0].rearrange("n p h d -> n p (h d)")}

        def load(eng, which, dst, sem, u, j):
            y = u & (NY - 1)
            first = (4 * ((u >> 3) & 1) + j) * NPAGES + (NY - 1) * PPC - y * PPC
            for i in range(PPC):
                page = eng.value_load(pages[0:1, ds(first + i, 1)], min_val=0, max_val=NPHYS - 1)
                eng.dma_start(dst[:, i, :], cache[which][ds(page, 1)].rearrange("a p n -> (a p) n")).then_inc(sem, 16)

        with nc.Block() as block:

            @block.sync
            def _(sp):
                sp.dma_start(pages[:, :], io["page_table"].rearrange("(a b) n -> a (b n)", a=1)).then_inc(s_pg, 16)
                sp.dma_start(v_new[:, :, :], io["v_sample"][0].rearrange("b t h d -> t b (h d)")).then_inc(s_small, 16)
                for j in range(4):
                    at = slice(32 * j, 32 * j + 32)
                    sp.dma_start(gain[at, :], io["norm_attn"][0].unsqueeze(1).to_broadcast([H, TS, DH])).then_inc(s_small, 16)
                    sp.dma_start(bias[at, :], io["sb_bias"][0].unsqueeze(1).unsqueeze(2).to_broadcast([H, TS, 1])).then_inc(s_small, 16)
                sp.wait_ge(s_pg, 16)
                for j in range(4):
                    load(sp, "k", kp[j], s_k[j], 0, j)
                hold(sp, s_kt, 1, s_sp)
                load(sp, "k", kp[0], s_k[0], 1, 0)
                with sp.Fori(0, NU) as u:
                    turned = [sp.snap(4 * u + 1 + m) for m in (1, 2, 3, 4)]
                    one, two = sp.snap((u + 1) & (NU - 1)), sp.snap((u + 2) & (NU - 1))

                    def load_k(j, at, n):
                        hold(sp, s_kt, turned[n], s_sp)
                        load(sp, "k", kp[j], s_k[j], at, j)

                    load_k(1, one, 0)
                    load_k(2, one, 1)
                    load_k(3, one, 2)
                    load_k(0, two, 3)
                for j in range(4):
                    sp.wait_ge(s_k[j], 64 * (NU + 1 + (j == 0)))

            @block.gpsimd
            def _(pool):
                for t in (tok, low, band):
                    pool.memset(t[:, :] if t is not band else t[:, :, :], 0.0 if t is not band else 1.0)
                pool.drain()
                pool.affine_select(out=tok[:, :].rearrange("t (a b) -> t a b", b=TS), in_=tok[:, :].rearrange("t (a b) -> t a b", b=TS),
                                   compare_op=ALU.not_equal, fill=1.0, base=0, pattern=[[0, P // TS], [1, TS]], channel_multiplier=-1)
                pool.affine_select(out=low[:, :], in_=low[:, :], compare_op=ALU.is_gt, fill=-1.0e30, base=0,
                                   pattern=[[-1, TS]], channel_multiplier=1)
                pool.affine_select(out=band[:, :, :], in_=band[:, :, :], compare_op=ALU.is_ge, fill=0.0, base=0,
                                   pattern=[[-32, 4], [-TS, H]], channel_multiplier=1)
                pool.drain()
                pool.affine_select(out=band[:, :, :], in_=band[:, :, :], compare_op=ALU.is_ge, fill=0.0, base=TS - 1,
                                   pattern=[[32, 4], [TS, H]], channel_multiplier=-1)
                pool.drain().then_inc(s_set, 1)

                def weights(v, out, a, b):
                    pool.wait_ge(s_scan, v + 1)
                    if not (isinstance(v, int) and v == 0):
                        pool.wait_ge(s_tw, v)
                    pool.tensor_tensor(out, a, b, ALU.mult).then_inc(s_w, 1)

                pool.wait_ge(s_pg, 16)
                for hb in range(2):
                    weights(9 * hb, w_n[:, :], take_n[:, :], left_n[:, 1:])
                    with pool.Fori(0, NY) as y:
                        u = 8 * hb + y
                        for j in range(4):
                            hold(pool, s_pv, 4 * u + 1 + j, s_sp)
                            load(pool, "v", vp[j], s_v[j], u, j)
                        weights(9 * hb + 1 + y, w[:, :], take[:, :], left[:, 1:])

            @block.scalar
            def _(act):
                act.wait_ge(s_nb, 1)

                def evac(m, zcount, j):
                    act.wait_ge(s_kt, m + 1)
                    act.wait_ge(s_z, zcount)
                    act.activation(kTs[j % 2][:, 2, :], kb[2][:, :], ACT.Copy)
                    act.activation(kTs[j % 2][:, 3, :], kb[3][:, :], ACT.Copy).then_inc(s_ka, 1)

                def sigmoids(v, ready, a, b, n):
                    act.wait_ge(s_z, ready)
                    if not (isinstance(v, int) and v == 0):
                        act.wait_ge(s_w, v)
                    act.activation(a, zb[:, 0:n], ACT.Sigmoid, scale=-SCALE, bias=nbias[:, 0:1])
                    act.activation(b, zb[:, 0:n], ACT.Sigmoid, scale=SCALE, bias=bias[:, 0:1]).then_inc(s_sg, 1)

                evac(0, 1, 0)
                for hb in range(2):
                    sigmoids(9 * hb, 2 + 33 * hb + 1, leave_n[:, :], take_n[:, :], TS)
                    with act.Fori(0, NY) as y:
                        u = 8 * hb + y
                        for j in (1, 2, 3, 4):
                            evac(4 * u + j, 4 * u + j + 2 + hb, j)
                        sigmoids(9 * hb + 1 + y, 2 + 4 * u + 4 + hb + 1, leave[:, :], take[:, :], CH)
                    act.wait_ge(s_os, hb + 1)
                    act.activation(o_sq[:, :], o_row[:, :], ACT.Square, scale=1.0 / math.sqrt(DH), accum_out=ssq[:, 0:1])
                    act.drain()
                    act.activation(ssq[:, 0:1], ssq[:, 0:1], ACT.Sqrt, bias=keep["eps"][:, 0:1]).then_inc(s_rs, 1)

            @block.tensor
            def _(pe):
                pe.wait_ge(s_small, 16 * 9)
                pe.wait_ge(s_set, 1)
                pe.nop().then_inc(s_z, 2)
                pe.nop().then_inc(s_pv, 4)

                def turn(m, j, u):
                    pe.wait_ge(s_k[j], 64 * u + 64)
                    if not (isinstance(m, int) and m == 0):
                        pe.wait_ge(s_kd, m)
                        pe.wait_ge(s_ka, m)
                    for f in range(FC):
                        for i in range(PPC):
                            mm = pe.transpose(kb[f][:, i * P:i * P + P], kp[j][:, i, f * P:f * P + P], ident[:, :])
                    mm.then_inc(s_kt, 1)

                def scores(hb, u, j):
                    pe.wait_ge(s_kd, 4 * u + j + 1)
                    pe.wait_ge(s_ka, 4 * u + j + 1)
                    if j == 0:
                        pe.wait_ge(s_sg, u + hb + 1)
                    for f in range(FC):
                        mm = pe.matmul(zb[32 * j:32 * j + 32, :], keep["q_blk"][:, 4 * hb + j, f, :], kTs[j % 2][:, f, :],
                                       start=(f == 0), stop=(f == FC - 1), skip_group_check=True)
                    mm.then_inc(s_z, 1)

                def turn_weights(v):
                    pe.wait_ge(s_w, v + 1)
                    pe.wait_ge(s_wt, v)
                    for i in range(PPC):
                        mm = pe.transpose(wb[:, i * P:i * P + P], w[:, i * P:i * P + P], ident[:, :])
                    mm.then_inc(s_tw, 1)

                def values(hb, u, j):
                    pe.wait_ge(s_v[j], 64 * u + 64)
                    if j == 0:
                        pe.wait_ge(s_wt, u + hb + 2)
                    for i in range(PPC):
                        mm = pe.matmul(ob[32 * j:32 * j + 32, :], wT[:, i, 32 * j:32 * j + 32], vp[j][:, i, :],
                                       start=False, stop=False, skip_group_check=True)
                    mm.then_inc(s_pv, 1)

                def step(hb, u, first):
                    turn(4 * u + 1, 1, u)
                    if not first:
                        turn_weights(u + hb)
                    scores(hb, u, 0)
                    for j in (1, 2, 3):
                        turn(4 * u + j + 1, (j + 1) % 4, u + (j == 3))
                        if not first:
                            values(hb, u - 1, j - 1)
                        scores(hb, u, j)
                    if not first:
                        values(hb, u - 1, 3)

                turn(0, 0, 0)
                for hb in range(2):
                    if hb:
                        pe.wait_ge(s_sg, 9 * hb)
                    for j in range(4):
                        b = 4 * hb + j
                        for f in range(FC):
                            pe.matmul(zb[32 * j:32 * j + 32, 0:TS], keep["q_blk"][:, b, f, :], keep["kT_new"][:, f, TS * b:TS * b + TS],
                                      start=(f == 0), stop=False, skip_group_check=True)
                    pe.matmul(zb[:, 0:TS], tok[:, :], low[:, :], start=False, stop=True, skip_group_check=True).then_inc(s_z, 1)
                    pe.wait_ge(s_w, 9 * hb + 1)
                    if hb:
                        pe.wait_ge(s_wt, 9 * hb)
                        pe.wait_ge(s_o, hb)
                    pe.transpose(wb[0:TS, 0:P], w_n[:, :], ident[:, :]).then_inc(s_tw, 1)
                    pe.wait_ge(s_wt, 9 * hb + 1)
                    for j in range(4):
                        pe.matmul(ob[32 * j:32 * j + 32, :], wT_n[:, 32 * j:32 * j + 32], v_new[:, 4 * hb + j, :],
                                  start=True, stop=False, skip_group_check=True)
                    step(hb, NY * hb, True)
                    with pe.Fori(1, NY) as y:
                        step(hb, NY * hb + y, False)
                    u = NY * hb + NY - 1
                    turn_weights(u + hb + 1)
                    for j in range(4):
                        values(hb, u, j)
                    pe.wait_ge(s_on, hb + 1)
                    pe.transpose(wb[0:DH, 0:P], o_row[:, :], ident[:, :]).then_inc(s_oT, 1)

            @block.vector
            def _(dve):
                dve.wait_ge(s_small, 16 * 9)
                dve.wait_ge(s_set, 1)
                dve.tensor_scalar(nbias[:, :], bias[:, :], -1.0, None, ALU.mult).then_inc(s_nb, 1)
                dve.tensor_reduce(own[:, :], band[:, :, :].rearrange("p j h -> p h j"), AX_X, ALU.add)
                dve.memset(left_n[:, TS:], 1.0)
                dve.drain()

                def evac(m, zcount, j):
                    dve.wait_ge(s_kt, m + 1)
                    dve.wait_ge(s_z, zcount)
                    dve.tensor_copy(kTs[j % 2][:, 0, :], kb[0][:, :])
                    dve.tensor_copy(kTs[j % 2][:, 1, :], kb[1][:, :]).then_inc(s_kd, 1)

                def unturn(v, u):
                    dve.wait_ge(s_tw, v + 1)
                    dve.wait_ge(s_pv, 4 * u + 4)
                    dve.tensor_copy(wT[:, :, :], wb[:, :].rearrange("p (i q) -> p i q", i=PPC)).then_inc(s_wt, 1)

                def scan(v, carry):
                    dve.wait_ge(s_w, v)
                    dve.tensor_copy(left[:, CH:], carry)
                    dve.drain()
                    dve.wait_ge(s_sg, v + 1)
                    dve.tensor_tensor_scan(left[:, 0:CH][:, ::-1], leave[:, ::-1], leave[:, ::-1], left[:, CH:],
                                           ALU.mult, ALU.bypass).then_inc(s_scan, 1)

                def step(hb, u, first):
                    evac(4 * u + 1, 4 * u + 3 + hb, 1)
                    if not first:
                        unturn(u + hb, u - 1)
                    for j in (2, 3, 4):
                        evac(4 * u + j, 4 * u + j + 2 + hb, j)
                    scan(u + hb + 1, left_n[:, 0:1] if first else left[:, 0:1])

                evac(0, 1, 0)
                for hb in range(2):
                    dve.wait_ge(s_sg, 9 * hb + 1)
                    dve.tensor_tensor_scan(left_n[:, 0:TS][:, ::-1], leave_n[:, ::-1], leave_n[:, ::-1], left_n[:, TS:],
                                           ALU.mult, ALU.bypass).then_inc(s_scan, 1)
                    dve.wait_ge(s_tw, 9 * hb + 1)
                    dve.tensor_copy(wT_n[:, :], wb[0:TS, 0:P]).then_inc(s_wt, 1)
                    step(hb, NY * hb, True)
                    with dve.Fori(1, NY) as y:
                        step(hb, NY * hb + y, False)
                    u = NY * hb + NY - 1
                    unturn(u + hb + 1, u)
                    dve.wait_ge(s_pv, 4 + 4 * (u + 1))
                    dve.tensor_tensor(o_all[:, :, :], ob[:, :].rearrange("p (h d) -> p h d", h=H),
                                      own[:, :].unsqueeze(2).to_broadcast([P, H, DH]), ALU.mult).then_inc(s_o, 1)
                    dve.drain()
                    dve.tensor_reduce(o_row[:, :], o_all[:, :, :].rearrange("p h d -> p d h"), AX_X, ALU.add).then_inc(s_os, 1)
                    dve.wait_ge(s_rs, hb + 1)
                    dve.reciprocal(ssq[:, 1:2], ssq[:, 0:1])
                    dve.drain()
                    dve.scalar_tensor_tensor(out=o_row[:, :], in0=o_row[:, :], scalar=ssq[:, 1:2], in1=gain[:, :],
                                             op0=ALU.mult, op1=ALU.mult).then_inc(s_on, 1)
                    dve.wait_ge(s_oT, hb + 1)
                    src = wb[0:DH, 0:P].rearrange("d (j f two q) -> d two f j q", j=4, f=FC, two=2)
                    for par in range(2):
                        dst = keep["oT_new"][64 * par:64 * par + 64, :, :].rearrange("d f (b t) -> d f b t", b=BS)
                        dve.tensor_copy(dst[:, :, 4 * hb:4 * hb + 4, :], src[:, par])
                    dve.drain()


def router_phase(nc, io, keep):
    with ExitStack() as stack:
        k = Kit(nc, stack)
        w_out = k.sb("w_out", [P, KC, D])
        w_r = k.sb("w_r", [P, KC, NG + NE])
        b_r = k.sb("b_r", [P, NG + NE])
        nf_row = k.sb("nf_row", [P, D])
        spread = [k.sb(f"spread{i}", [P, P]) for i in range(2)]
        o_n, o_sq = k.sb("o_n", [P, WA]), k.sb("o_sq6", [P, WA])
        ss8 = k.sb("ss8", [P, H])
        featT = k.sb("featT", [P, KC, P])
        x_t = k.sb("x_t6", [P, D])
        t1, x1, t2, xn = (k.sb(n, [P, D]) for n in ("t1", "x1", "t2", "xn2"))
        junk = k.sb("junk6", [P, D], BF16)
        ssq = k.sb("ssq6", [P, 2])
        xT = k.sb("xT6", [P, KC, P])
        fill = k.sb("fill", [P, FILL, 4])
        tri, onesb = k.sb("tri", [P, P], BF16), k.sb("onesb", [P, P], BF16)
        iota = k.sb("iota", [P, NE])
        ebase, tok = k.sb("ebase", [P, NE]), k.sb("tok6", [P, 1])
        iota_i = k.sb("iota_i", [P, NE], I32)
        tok_i = k.sb("tok_i", [P, 1], I32)
        lg, g8, m8, v8, e8 = (k.sb(n, [P, c]) for n, c in (("lg", NG + NE), ("g8", 8), ("m8", 8), ("v8", 8), ("e8", 8)))
        gi, vi = k.sb("gi", [P, 8], U32), k.sb("vi", [P, 8], U32)
        gf, vf, nm, nv, sexp, e1, gates, den, dest = (
            k.sb(n, [P, c]) for n, c in (("gf", 1), ("vf", 2), ("nm", 1), ("nv", 1), ("sexp", 1), ("e1", 1), ("gates", 2),
                                         ("den", 1), ("dest", 2)))
        ex4 = k.sb("ex4", [P, NG])
        hot4, sel = k.sb("hot4", [P, NG]), k.sb("sel", [P, NG, EPG])
        hot = k.sb("hot", [P, 2, NE])
        both = k.sb("both", [P, NE], BF16)
        cnt, place, pick = k.sb("cnt", [P, NE]), k.sb("place", [P, NE]), k.sb("pick", [P, NE])
        slot = k.sb("slot", [P, 2])
        dest_u = k.sb("dest_u", [P, 2], U32)
        pay = k.sb("pay", [P, 2, 4])
        tb = k.ps("tb6", [P, 512])
        pb = [k.ps(f"pb6{i}", [P, 512]) for i in range(2)]
        xb = [k.ps(f"xb6{i}", [P, 512]) for i in range(2)]
        lb, cb = k.ps("lb6", [P, 512]), k.ps("cb6", [P, 512])
        s = {n: k.sem(f"p6_{n}") for n in ("w", "r", "x", "rg", "fill", "set", "sp", "oh", "os", "or", "on", "oT", "fe", "mm", "t1",
                                            "x1", "xs", "xr", "t2", "xn", "st1", "st2", "xT", "xe", "lg", "lo", "nm", "ex", "nv", "e1",
                                            "both", "cb", "dst", "sc", "scat", "rt", "spr", "spm", "spe", "done", "free")}
        ident, o_nat, modT = keep["ident"], keep["o_nat"], keep["modT"]
        rows = {P: keep["rowsP"], NS: keep["rowsS"]}
        rgT = io["rgT_d"].rearrange("(f p) (t q) -> t p f q", p=P, q=P)
        x_src = io["x_prompt"][0].rearrange("(t p) n -> t p n", p=P)
        table = io["table_d"]

        def size(t):
            return NS if isinstance(t, int) and t == NT else P

        def all_rounds(eng, a_round):
            a_round(0)
            a_round(1)
            with eng.Fori(2, NT - 1) as t:
                a_round(t)
            for t in range(NT - 1, NT + 3):
                a_round(t)

        def there(t, off, last=NT):
            return not isinstance(t, int) or 0 <= t + off <= last

        def tile_rows(t, n):
            return ds(t * P, n)

        with nc.Block() as block:

            @block.sync
            def _(sp):
                sp.dma_start(nf_row[:, :], io["norm_ffn"].to_broadcast([P, D])).then_inc(s["r"], 16)
                sp.dma_start(b_r[:, 0:NG], io["b_group"].to_broadcast([P, NG])).then_inc(s["r"], 16)
                sp.dma_start(b_r[:, NG:], io["b_router"].to_broadcast([P, NE])).then_inc(s["r"], 16)
                sp.dma_start(w_out[:, :, :], io["w_out"][0].rearrange("(c p) n -> p c n", p=P)).then_inc(s["w"], 16)
                sp.dma_start(w_r[:, :, 0:NG], io["w_group"][0].rearrange("(c p) n -> p c n", p=P)).then_inc(s["w"], 16)
                sp.dma_start(w_r[:, :, NG:], io["w_router"][0].rearrange("(c p) n -> p c n", p=P)).then_inc(s["w"], 16)
                sp.wait_ge(s["fill"], 1)
                tab = table.rearrange("(a p r) c -> a p (r c)", p=P, r=FILL)
                for a in range(NE * CAP // (P * FILL)):
                    sp.dma_start(tab[a], fill[:, :, :].rearrange("p r c -> p (r c)")).then_inc(s["scat"], 16)

                def loads(t, n):
                    if n == P:
                        sp.dma_start(featT[:, FC:, :], rgT[ds(t, 1)].rearrange("a p f q -> (a p) f q")).then_inc(s["rg"], 16)
                        sp.dma_start(x_t[:, :], x_src[ds(t, 1)].rearrange("a p n -> (a p) n")).then_inc(s["x"], 16)
                    else:
                        sp.dma_start(x_t[0:NS, :], io["x_sample"].rearrange("b t n -> (b t) n")).then_inc(s["x"], 16)

                def a_round(t, n_next):
                    one, n = t + 1, (NS if (isinstance(t, int) and t == NT) else P)
                    if not isinstance(t, int):
                        one = sp.snap(t + 1)
                        t = sp.snap(t + 0)
                    if n_next:
                        hold(sp, s["mm"], one, s["sp"])
                        hold(sp, s["x1"], one, s["sp"])
                        loads(one, n_next)
                    else:
                        hold(sp, s["x1"], one, s["sp"])
                    sp.dma_start(io["x1_d"][tile_rows(t, n), :], x1[0:n, :]).then_inc(s["st1"], 16)
                    hold(sp, s["xn"], one, s["sp"])
                    sp.dma_start(io["xn_d"][tile_rows(t, n), :], xn[0:n, :]).then_inc(s["st2"], 16)

                loads(0, P)
                with sp.Fori(0, NT - 1) as t:
                    a_round(t, P)
                a_round(NT - 1, NS)
                a_round(NT, 0)
                for name, n in (("st1", NT + 1), ("st2", NT + 1)):
                    sp.wait_ge(s[name], 16 * n)

            @block.gpsimd
            def _(pool):
                pool.iota(iota_i[:, :], pattern=[[1, NE]], base=0, channel_multiplier=0).then_inc(s["set"], 1)
                pool.iota(tok_i[:, :], pattern=[[0, 1]], base=0, channel_multiplier=1).then_inc(s["set"], 1)
                pool.memset(tri[:, :], 1.0)
                pool.memset(onesb[:, :], 1.0)
                pool.drain()
                pool.affine_select(out=tri[:, :], in_=tri[:, :], compare_op=ALU.is_gt, fill=0.0, base=0,
                                   pattern=[[1, P]], channel_multiplier=-1)
                pool.drain().then_inc(s["set"], 1)

                def stage_b(t, n):
                    pool.wait_ge(s["t1"], t + 1)
                    pool.wait_ge(s["x"], 16 * t + 16)
                    if not (isinstance(t, int) and t == 0):
                        pool.wait_ge(s["st1"], 16 * t)
                    pool.tensor_tensor(x1[0:n, :], t1[0:n, :], x_t[0:n, :], ALU.add).then_inc(s["x1"], 1)
                    pool.wait_ge(s["t2"], t + 1)
                    if not (isinstance(t, int) and t == 0):
                        pool.wait_ge(s["st2"], 16 * t)
                        pool.wait_ge(s["xT"], t)
                    pool.tensor_tensor(xn[0:n, :], t2[0:n, :], rows[n][0:n, 2, :], ALU.add).then_inc(s["xn"], 1)

                def stage_d(t, n):
                    hold(pool, s["dst"], t + 1, s["sp"])
                    if isinstance(t, int) and t == 0:
                        pool.wait_ge(s["scat"], 16 * (NE * CAP // (P * FILL)))
                    for i in range(2):
                        pool.indirect_dma_start(out=table, out_offset=bass.IndirectOffsetOnAxis(ap=dest_u[0:n, i:i + 1], axis=0),
                                                in_=pay[0:n, i, :], in_offset=None).then_inc(s["sc"], 16)

                def a_round(t):
                    if there(t, 0):
                        stage_b(t, size(t))
                    if there(t, -2):
                        stage_d(t - 2, size(t - 2))

                all_rounds(pool, a_round)
                pool.wait_ge(s["sc"], 32 * (NT + 1))

            @block.scalar
            def _(act):
                act.wait_ge(s["r"], 48)
                for i in range(16):
                    act.wait_ge(s["spm"], i + 1)
                    kind, half, n = i // 4, i // 2 % 2, (P, NS)[i % 2]
                    act.activation(rows[n][0:n, kind, half * 512:half * 512 + 512], pb[i % 2][0:n, :], ACT.Copy).then_inc(s["spe"], 1)

                def stage_a(t):
                    src = o_nat[:, :, :].rearrange("p t n -> p (t n)")[:, ds(t * WA, WA)]
                    act.drain()
                    if not (isinstance(t, int) and t == 0):
                        hold(act, s["os"], t, s["sp"])
                    act.activation(o_sq[:, :], src, ACT.Square, scale=1.0 / math.sqrt(DH)).then_inc(s["oh"], 1)
                    act.wait_ge(s["os"], t + 1)
                    act.activation(ss8[:, :], ss8[:, :], ACT.Sqrt, bias=keep["eps"][:, 0:1]).then_inc(s["or"], 1)

                def stage_b(t, n):
                    act.wait_ge(s["x1"], t + 1)
                    act.activation(junk[0:n, :], x1[0:n, :], ACT.Square, scale=1.0 / math.sqrt(D), accum_out=ssq[0:n, 0:1])
                    act.drain()
                    act.activation(ssq[0:n, 0:1], ssq[0:n, 0:1], ACT.Sqrt, bias=keep["eps"][0:n, 0:1]).then_inc(s["xs"], 1)

                def rows_turned(t, n):
                    act.wait_ge(s["xT"], t + 1)
                    for i in range(2):
                        last = act.activation(xT[:, 4 * i:4 * i + 4, 0:n], xb[i][:, 0:4 * n].rearrange("p (c n) -> p c n", c=4), ACT.Copy)
                    last.then_inc(s["xe"], 1)

                def stage_c(t, n):
                    act.wait_ge(s["nm"], t + 1)
                    act.activation(ex4[0:n, :], lg[0:n, 0:NG], ACT.Exp, bias=nm[0:n, 0:1], accum_out=sexp[0:n, 0:1]).then_inc(s["ex"], 1)
                    act.wait_ge(s["nv"], t + 1)
                    act.activation(e1[0:n, :], v8[0:n, 1:2], ACT.Exp, bias=nv[0:n, 0:1]).then_inc(s["e1"], 1)

                def a_round(t):
                    if there(t, 1, NT - 1):
                        stage_a(t + 1)
                    if there(t, -1):
                        rows_turned(t - 1, size(t - 1))
                    if there(t, 0):
                        stage_b(t, size(t))
                    if there(t, -1):
                        stage_c(t - 1, size(t - 1))

                stage_a(0)
                all_rounds(act, a_round)

            @block.tensor
            def _(pe):
                for i in range(16):
                    kind, half, n = i // 4, i // 2 % 2, (P, NS)[i % 2]
                    if i >= 2:
                        pe.wait_ge(s["spe"], i - 1)
                    for c in range(4):
                        pe.wait_ge(s["spr"], 4 * i + c + 1)
                        mm = pe.matmul(pb[i % 2][0:n, c * P:c * P + P], spread[c % 2][:, 0:n], ident[:, :], start=True, stop=True)
                        mm.then_inc(s["rt"], 1)
                    pe.drain().then_inc(s["spm"], 1)
                pe.wait_ge(s["spe"], 16)
                pe.wait_ge(s["set"], 3)
                pe.wait_ge(s["w"], 48)

                def stage_a(t):
                    pe.wait_ge(s["on"], t + 1)
                    for f in range(FC):
                        mm = pe.transpose(tb[:, f * P:f * P + P], o_n[:, f * P:f * P + P], ident[:, :])
                    mm.then_inc(s["oT"], 1)

                def stage_b(t, n):
                    pe.wait_ge(s["fe"], t + 1)
                    if n == P:
                        pe.wait_ge(s["rg"], 16 * t + 16)
                    if not (isinstance(t, int) and t == 0):
                        pe.wait_ge(s["t1"], t)
                    for half in range(2):
                        for c in range(KC):
                            mm = pe.matmul(pb[half][0:n, :], featT[:, c, 0:n], w_out[:, c, half * 512:half * 512 + 512],
                                           start=(c == 0), stop=(c == KC - 1))
                    mm.then_inc(s["mm"], 1)

                def turn_rows(t, n):
                    pe.wait_ge(s["xn"], t + 1)
                    for c in range(KC):
                        mm = pe.transpose(xb[c // 4][:, (c % 4) * n:(c % 4) * n + n], xn[0:n, c * P:c * P + P], ident[0:n, 0:n])
                    mm.then_inc(s["xT"], 1)

                def stage_c(t, n):
                    pe.wait_ge(s["xe"], t + 1)
                    for c in range(KC):
                        mm = pe.matmul(lb[0:n, 0:NG + NE], xT[:, c, 0:n], w_r[:, c, :], start=(c == 0), stop=(c == KC - 1))
                    mm.then_inc(s["lg"], 1)

                def stage_d(t, n):
                    pe.wait_ge(s["both"], t + 1)
                    pe.matmul(cb[0:n, 0:NE], tri[0:n, 0:n], both[0:n, :], start=True, stop=True)
                    pe.matmul(cb[:, 64:64 + NE], onesb[0:n, :], both[0:n, :], start=True, stop=True).then_inc(s["cb"], 1)

                def a_round(t):
                    if there(t, 0):
                        stage_b(t, size(t))
                    if there(t, 1, NT - 1):
                        stage_a(t + 1)
                    if there(t, -1):
                        turn_rows(t - 1, size(t - 1))
                    if there(t, -2):
                        stage_d(t - 2, size(t - 2))
                    if there(t, -1):
                        stage_c(t - 1, size(t - 1))

                stage_a(0)
                all_rounds(pe, a_round)

            @block.vector
            def _(dve):
                for j in range(64):
                    i, c = j // 4, j % 4
                    kind, half, n = i // 4, i // 2 % 2, (P, NS)[i % 2]
                    chunk = (GATE1, SCALE2, SHIFT2, GATE2)[kind] + 4 * half + c
                    if j >= 2:
                        dve.wait_ge(s["rt"], j - 1)
                    if n == P:
                        dve.tensor_copy(spread[c % 2][:, :], modT[:, chunk, 0:1].to_broadcast([P, P])).then_inc(s["spr"], 1)
                    else:
                        dve.tensor_copy(spread[c % 2][:, 0:NS].rearrange("p (b t) -> p b t", b=BS),
                                        modT[:, chunk, 1:].unsqueeze(2).to_broadcast([P, BS, TS])).then_inc(s["spr"], 1)
                dve.wait_ge(s["spe"], 16)
                dve.wait_ge(s["r"], 48)
                for n in (P, NS):
                    dve.scalar_tensor_tensor(out=rows[n][0:n, 1, :], in0=rows[n][0:n, 1, :], scalar=1.0, in1=nf_row[0:n, :],
                                             op0=ALU.add, op1=ALU.mult)
                dve.wait_ge(s["set"], 3)
                dve.tensor_copy(iota[:, :], iota_i[:, :])
                dve.tensor_copy(tok[:, :], tok_i[:, :])
                dve.memset(cnt[:, :], 0.0)
                dve.memset(g8[:, :], -3.0e38)
                dve.memset(pay[:, :, :], 0.0)
                dve.memset(fill[:, :, :], 0.0)
                dve.drain()
                dve.memset(fill[:, :, 1:2].bitcast(U32), NO_ROW)
                dve.tensor_scalar(ebase[:, :], iota[:, :], float(CAP), None, ALU.mult)
                dve.drain().then_inc(s["fill"], 1)

                def stage_a1(t):
                    dve.drain()
                    dve.wait_ge(s["oh"], t + 1)
                    dve.tensor_reduce(ss8[:, :], o_sq[:, :].rearrange("p (h d) -> p h d", h=H), AX_X, ALU.add).then_inc(s["os"], 1)
                    dve.wait_ge(s["or"], t + 1)
                    dve.reciprocal(ss8[:, :], ss8[:, :])
                    dve.drain()
                    if not (isinstance(t, int) and t == 0):
                        dve.wait_ge(s["oT"], t)
                    src = o_nat[:, :, :].rearrange("p t n -> p (t n)")[:, ds(t * WA, WA)].rearrange("p (h d) -> p h d", h=H)
                    dve.tensor_tensor(o_n[:, :].rearrange("p (h d) -> p h d", h=H), src,
                                      ss8[:, :].unsqueeze(2).to_broadcast([P, H, DH]), ALU.mult).then_inc(s["on"], 1)

                def stage_a2(t):
                    dve.wait_ge(s["oT"], t + 1)
                    if not (isinstance(t, int) and t == 0):
                        dve.wait_ge(s["mm"], t)
                    r = VEC_ROWS["norm_attn"][0]
                    for f in range(FC):
                        last = dve.tensor_scalar(featT[:, f, :], tb[:, f * P:f * P + P], keep["vecT"][:, r + f:r + f + 1], None, ALU.mult)
                    last.then_inc(s["fe"], 1)

                def stage_b(t, n):
                    dve.wait_ge(s["mm"], t + 1)
                    for half in range(2):
                        cols = slice(half * 512, half * 512 + 512)
                        last = dve.tensor_tensor(t1[0:n, cols], pb[half][0:n, :], rows[n][0:n, 0, cols], ALU.mult)
                    last.then_inc(s["t1"], 1)

                def stage_b2(t, n):
                    dve.wait_ge(s["xs"], t + 1)
                    dve.reciprocal(ssq[0:n, 1:2], ssq[0:n, 0:1])
                    dve.drain()
                    dve.scalar_tensor_tensor(out=t2[0:n, :], in0=x1[0:n, :], scalar=ssq[0:n, 1:2], in1=rows[n][0:n, 1, :],
                                             op0=ALU.mult, op1=ALU.mult)
                    dve.drain().then_inc(s["t2"], 1)

                def stage_c(t, n):
                    p = slice(0, n)
                    dve.wait_ge(s["lg"], t + 1)
                    dve.tensor_tensor(lg[p, :], lb[p, 0:NG + NE], b_r[p, :], ALU.add)
                    dve.drain()
                    dve.tensor_copy(g8[p, 0:NG], lg[p, 0:NG])
                    dve.drain()
                    dve.max(m8[p, :], g8[p, :])
                    dve.drain()
                    dve.max_index(gi[p, :], m8[p, :], g8[p, :])
                    dve.tensor_scalar(nm[p, :], m8[p, 0:1], -1.0, None, ALU.mult).then_inc(s["nm"], 1)
                    dve.drain()
                    dve.tensor_copy(gf[p, :], gi[p, 0:1])
                    dve.drain()
                    dve.tensor_scalar(hot4[p, :], iota[p, 0:NG], gf[p, 0:1], None, ALU.is_equal)
                    dve.drain()
                    dve.tensor_tensor(sel[p, :, :], lg[p, NG:].rearrange("p (g e) -> p g e", g=NG),
                                      hot4[p, :].unsqueeze(2).to_broadcast([n, NG, EPG]), ALU.mult)
                    dve.drain()
                    dve.tensor_reduce(e8[p, :], sel[p, :, :].rearrange("p g e -> p e g"), AX_X, ALU.add)
                    dve.drain()
                    dve.max(v8[p, :], e8[p, :])
                    dve.drain()
                    dve.max_index(vi[p, :], v8[p, :], e8[p, :])
                    dve.tensor_scalar(nv[p, :], v8[p, 0:1], -1.0, None, ALU.mult).then_inc(s["nv"], 1)
                    dve.drain()
                    dve.tensor_copy(vf[p, :], vi[p, 0:2])
                    dve.drain()
                    dve.scalar_tensor_tensor(out=vf[p, :], in0=gf[p, 0:1].to_broadcast([n, 2]), scalar=float(EPG), in1=vf[p, :],
                                             op0=ALU.mult, op1=ALU.add)
                    dve.drain()
                    for i in range(2):
                        dve.tensor_scalar(hot[p, i, :], iota[p, :], vf[p, i:i + 1], None, ALU.is_equal)
                    dve.drain()
                    if not (isinstance(t, int) and t == 0):
                        dve.wait_ge(s["cb"], t)
                    dve.tensor_tensor(both[p, :], hot[p, 0, :], hot[p, 1, :], ALU.add).then_inc(s["both"], 1)

                def stage_d(t, n):
                    p = slice(0, n)
                    dve.wait_ge(s["ex"], t + 1)
                    dve.wait_ge(s["e1"], t + 1)
                    dve.scalar_tensor_tensor(out=den[p, :], in0=e1[p, :], scalar=1.0, in1=sexp[p, :], op0=ALU.add, op1=ALU.mult)
                    dve.drain()
                    if not (isinstance(t, int) and t == 0):
                        dve.wait_ge(s["sc"], 32 * t)
                    dve.reciprocal(pay[p, 0, 2:3], den[p, :])
                    dve.drain()
                    dve.tensor_tensor(pay[p, 1, 2:3], pay[p, 0, 2:3], e1[p, :], ALU.mult)
                    dve.wait_ge(s["cb"], t + 1)
                    dve.tensor_tensor(place[p, :], cb[p, 0:NE], cnt[p, :], ALU.add)
                    dve.drain()
                    dve.tensor_tensor(place[p, :], place[p, :], ebase[p, :], ALU.add)
                    dve.tensor_tensor(cnt[:, :], cnt[:, :], cb[:, 64:64 + NE], ALU.add)
                    for i in range(2):
                        dve.drain()
                        dve.tensor_tensor_reduce(pick[p, :], hot[p, i, :], place[p, :], 1.0, 0.0, ALU.mult, ALU.add, dest[p, i:i + 1])
                        dve.tensor_scalar(slot[p, i:i + 1], tok[p, :], 2.0, float(i), ALU.mult, ALU.add)
                    dve.drain()
                    dve.tensor_copy(dest_u[p, :], dest[p, :])
                    for i in range(2):
                        dve.tensor_copy(pay[p, i, 0:1].bitcast(U32), tok[p, :])
                        dve.tensor_copy(pay[p, i, 1:2].bitcast(U32), slot[p, i:i + 1])
                    dve.drain().then_inc(s["dst"], 1)
                    dve.tensor_scalar(tok[:, :], tok[:, :], float(P), None, ALU.add)
                    dve.drain()

                def sample_features():
                    dve.wait_ge(s["mm"], NT)
                    dve.tensor_copy(featT[:, 0:FC, 0:NS], keep["oT_new"][:, :, :])
                    dve.tensor_copy(featT[:, FC:, 0:NS], keep["rgT_new"][:, :, :])
                    dve.drain().then_inc(s["fe"], 1)

                def a_round(t):
                    if there(t, 1, NT - 1):
                        stage_a1(t + 1)
                    if there(t, 0):
                        stage_b(t, size(t))
                    if there(t, 1, NT - 1):
                        stage_a2(t + 1)
                    elif t == NT - 1:
                        sample_features()
                    if there(t, -2):
                        stage_d(t - 2, size(t - 2))
                    if there(t, 0):
                        stage_b2(t, size(t))
                    if there(t, -1):
                        stage_c(t - 1, size(t - 1))

                stage_a1(0)
                stage_a2(0)
                all_rounds(dve, a_round)
                dve.tensor_scalar(place[:, :], cnt[:, :], 1.0 / P, float(P - 1) / P - 0.5 + 1.0 / (2 * P), ALU.mult, ALU.add)
                dve.drain()
                dve.tensor_scalar(place[:, :], place[:, :], 1.0, None, ALU.max)
                dve.drain()
                dve.tensor_copy(keep["n_blocks"][:, :], place[0:1, :])
                dve.drain()


def experts_phase(nc, io, keep):
    with ExitStack() as stack:
        k = Kit(nc, stack)
        w13 = [k.sb(f"w13_{i}", [P, KC, 2, 2, DE // 2]) for i in range(2)]
        w2 = [k.sb(f"w2_{i}", [P, EC, D]) for i in range(2)]
        entry, entry_next, entry_run, entry_out = (k.sb(n, [P, 4]) for n in ("entry", "entry_next", "entry_run", "entry_out"))
        rows_in = k.sb("rows_in", [P, D])
        xT = k.sb("xT7", [P, KC, P])
        sg, hid = k.sb("sg7", [P, 2, DE // 2]), k.sb("hid", [P, DE])
        hT = k.sb("hT", [P, EC, P])
        y = k.sb("y7", [P, D])
        xb, yb = k.ps("xb7", [P, D]), k.ps("yb7", [P, D])
        h = [k.ps(f"h7_{half}", [P, 2, DE // 2]) for half in range(2)]
        tb = k.ps("tb7", [P, 512])
        s = {n: k.sem(f"p7_{n}") for n in ("ent", "in", "run", "xT", "xe", "h", "sg", "hid", "hT", "he", "y", "ye", "sc", "sp",
                                            "used", "go")}
        s_wt = [k.sem(f"p7_wt{i}") for i in range(2)]
        ident = keep["ident"]
        src = {n: io[n][0] for n in ("w1", "w3", "w2")}
        table, xn, yd = io["table_d"], io["xn_d"], io["y_d"]

        def experts(eng, body, before=None, after=None):
            count = eng.alloc_register(f"blocks_{eng.engine.name}")
            eng.reg_mov(count, 0)
            with eng.Fori(0, NE // 2) as pair:
                for i in range(2):
                    e = eng.snap(2 * pair + i)
                    blocks = eng.value_load(keep["n_blocks"][0:1, ds(e, 1)], min_val=1, max_val=CAP // P)
                    if before:
                        before(i, pair)
                    with eng.Fori(0, blocks) as b:
                        body(i, eng.snap(count, min_val=0, max_val=MAX_BLOCKS), e, b)
                        eng.reg_add(count, count, 1)
                    if after:
                        after()
            return eng.snap(count, min_val=NE, max_val=MAX_BLOCKS)

        with nc.Block() as block:

            @block.sync
            def _(sp):
                with sp.Fori(0, NE // 2) as pair:
                    for i in range(2):
                        e, free = sp.snap(2 * pair + i), sp.snap(2 * pair + i + 1)
                        hold(sp, s["used"], free, s["sp"])
                        for at, name in enumerate(("w1", "w3")):
                            w = src[name][ds(e, 1)].rearrange("a (c p) (half n) -> p (a c) half n", p=P, half=2)
                            for half in range(2):
                                sp.dma_start(w13[i][:, :, half, at, :], w[:, :, half, :]).then_inc(s_wt[i], 16)
                        sp.dma_start(w2[i][:, :, :], src["w2"][ds(e, 1)].rearrange("a (c p) n -> p (a c) n", p=P)).then_inc(s_wt[i], 16)

            @block.gpsimd
            def _(pool):
                pool.nop().then_inc(s["used"], 2)
                pool.nop().then_inc(s["ye"], 2)
                pool.nop().then_inc(s["run"], 1)
                pool.nop().then_inc(s["xT"], 1)
                pool.wait_ge(s["go"], 1)

                def scatter(n):
                    hold(pool, s["ye"], n + 1, s["sp"])
                    pool.indirect_dma_start(out=yd, out_offset=bass.IndirectOffsetOnAxis(ap=entry_out[:, 1:2].bitcast(U32), axis=0),
                                            in_=y[:, :], in_offset=None, bounds_check=2 * NTOK - 1, oob_is_err=False).then_inc(s["sc"], 16)

                def a_round(n, row):
                    hold(pool, s["run"], n + 1, s["sp"])
                    hold(pool, s["xT"], n + 1, s["sp"])
                    pool.dma_start(entry[:, :], table[ds(row, P), :]).then_inc(s["ent"], 16)
                    hold(pool, s["ent"], 16 * n + 16, s["sp"])
                    pool.indirect_dma_start(out=rows_in[:, :], out_offset=None, in_=xn,
                                            in_offset=bass.IndirectOffsetOnAxis(ap=entry[:, 0:1].bitcast(U32), axis=0)).then_inc(s["in"], 16)
                    scatter(n)

                n = experts(pool, lambda i, n, e, b: a_round(n, pool.snap(e * CAP + b * P)))
                a_round(n, 0)
                scatter(n + 1)
                hold(pool, s["sc"], 16 * n + 32, s["sp"])
                hold(pool, s["in"], 16 * n + 16, s["sp"])

            @block.scalar
            def _(act):
                def turned(n):
                    act.wait_ge(s["xT"], n + 2)
                    act.activation(xT[:, :, :], xb[:, :].rearrange("p (c n) -> p c n", c=KC), ACT.Copy).then_inc(s["xe"], 1)

                def body(i, n, e, b):
                    for half in range(2):
                        act.wait_ge(s["h"], 2 * n + half + 1)
                        act.activation(sg[:, half, :], h[half][:, 0, :], ACT.Sigmoid).then_inc(s["sg"], 1)
                    turned(n + 1)

                turned(0)
                experts(act, body)

            @block.tensor
            def _(pe):
                def turn(n):
                    pe.wait_ge(s["in"], 16 * n + 16)
                    for c in range(KC):
                        mm = pe.transpose(xb[:, c * P:c * P + P], rows_in[:, c * P:c * P + P], ident[:, :])
                    mm.then_inc(s["xT"], 1)

                def turn_hidden(n, half):
                    pe.wait_ge(s["hid"], 2 * n + half + 1)
                    for c in range(2 * half, 2 * half + 2):
                        mm = pe.transpose(tb[:, c * P:c * P + P], hid[:, c * P:c * P + P], ident[:, :])
                    mm.then_inc(s["hT"], 1)

                def out(i, cols, half):
                    for c in range(2 * half, 2 * half + 2):
                        mm = pe.matmul(yb[:, cols * 512:cols * 512 + 512], hT[:, c, :], w2[i][:, c, cols * 512:cols * 512 + 512],
                                       start=(c == 0), stop=(c == EC - 1))
                    return mm

                def body(i, n, e, b):
                    pe.wait_ge(s["xe"], n + 1)
                    for half in range(2):
                        for c in range(KC):
                            mm = pe.matmul(h[half][:, :, :], xT[:, c, :], w13[i][:, c, half, :, :], start=(c == 0), stop=(c == KC - 1))
                        mm.then_inc(s["h"], 1)
                    turn_hidden(n, 0)
                    turn(n + 1)
                    pe.wait_ge(s["he"], 2 * n + 1)
                    out(i, 0, 0)
                    turn_hidden(n, 1)
                    out(i, 1, 0)
                    pe.wait_ge(s["he"], 2 * n + 2)
                    out(i, 0, 1)
                    out(i, 1, 1).then_inc(s["y"], 1)

                turn(0)
                experts(pe, body, before=lambda i, pair: hold(pe, s_wt[i], 80 * pair + 80, s["sp"]),
                        after=lambda: pe.drain().then_inc(s["used"], 1))

            @block.vector
            def _(dve):
                dve.memset(y[:, :], 0.0)
                dve.memset(entry_out[:, :].bitcast(U32), NO_ROW)
                dve.drain().then_inc(s["go"], 1)

                def arrived(n):
                    dve.wait_ge(s["ent"], 16 * n + 16)
                    dve.wait_ge(s["in"], 16 * n + 16)
                    dve.tensor_copy(entry_next[:, :].bitcast(U32), entry[:, :].bitcast(U32)).then_inc(s["run"], 1)

                def body(i, n, e, b):
                    dve.tensor_copy(entry_run[:, :].bitcast(U32), entry_next[:, :].bitcast(U32))

                    def silu(half):
                        dve.wait_ge(s["sg"], 2 * n + half + 1)
                        dve.tensor_tensor(sg[:, half, :], sg[:, half, :], h[half][:, 0, :], ALU.mult)
                        dve.drain()
                        dve.tensor_tensor(hid[:, half * 256:half * 256 + 256], sg[:, half, :], h[half][:, 1, :], ALU.mult).then_inc(s["hid"], 1)

                    def turned(half):
                        dve.wait_ge(s["hT"], 2 * n + half + 1)
                        dve.tensor_copy(hT[:, 2 * half:2 * half + 2, :], tb[:, half * 256:half * 256 + 256].rearrange("p (c n) -> p c n", c=2)).then_inc(s["he"], 1)

                    silu(0)
                    turned(0)
                    silu(1)
                    arrived(n + 1)
                    turned(1)
                    dve.wait_ge(s["sc"], 16 * n + 32)
                    dve.tensor_copy(entry_out[:, :].bitcast(U32), entry_run[:, :].bitcast(U32))
                    dve.wait_ge(s["y"], n + 1)
                    dve.tensor_scalar(y[:, :], yb[:, :], entry_run[:, 2:3], None, ALU.mult)
                    dve.drain().then_inc(s["ye"], 1)

                arrived(0)
                dve.drain()
                experts(dve, body)


def final_phase(nc, io, keep):
    SETS = 4
    with ExitStack() as stack:
        k = Kit(nc, stack)
        f_row = k.sb("f_row", [P, D])
        x1 = [k.sb(f"x1_8{i}", [P, D]) for i in range(SETS)]
        yy = [k.sb(f"yy{i}", [P, 2, D]) for i in range(SETS)]
        out = [k.sb(f"out8{i}", [P, D]) for i in range(SETS)]
        junk = k.sb("junk8", [P, D], BF16)
        ssq = [k.sb(f"ssq8{i}", [P, 2]) for i in range(SETS)]
        s = {n: k.sem(f"p8_{n}") for n in ("f", "sum", "x2", "sq", "out", "sp")}
        s_in = [k.sem(f"p8_in{i}") for i in range(SETS)]
        s_st = [k.sem(f"p8_st{i}") for i in range(SETS)]
        rows = {P: keep["rowsP"], NS: keep["rowsS"]}
        y_out = io["y_prompt"][0]
        yd = io["y_d"].rearrange("(t two) n -> t two n", two=2)

        with nc.Block() as block:

            @block.sync
            def _(sp):
                sp.dma_start(f_row[:, :], io["final_norm"].rearrange("(a n) -> a n", a=1).to_broadcast([P, D])).then_inc(s["f"], 16)

                def load(t, i, n):
                    sp.dma_start(x1[i][0:n, :], io["x1_d"][ds(t * P, n), :]).then_inc(s_in[i], 16)
                    sp.dma_start(yy[i][0:n, :, :], yd[ds(t * P, n)]).then_inc(s_in[i], 16)

                for i in range(SETS):
                    load(i, i, P)
                with sp.Fori(0, NT // SETS - 1) as r:
                    for i in range(SETS):
                        t, done, nxt = sp.snap(SETS * r + i), sp.snap(SETS * r + i + 1), sp.snap(SETS * r + i + SETS)
                        hold(sp, s["out"], done, s["sp"])
                        sp.dma_start(y_out[ds(t * P, P), :], out[i][:, :]).then_inc(s_st[i], 16)
                        load(nxt, i, P)
                for i in range(SETS):
                    t = NT - SETS + i
                    sp.wait_ge(s["out"], t + 1)
                    sp.dma_start(y_out[t * P:t * P + P, :], out[i][:, :]).then_inc(s_st[i], 16)
                    if i == 0:
                        load(NT, 0, NS)
                sp.wait_ge(s["out"], NT + 1)
                sp.dma_start(io["y_sample"].rearrange("b t n -> (b t) n"), out[0][0:NS, :]).then_inc(s_st[0], 16)
                for i in range(SETS):
                    sp.wait_ge(s_st[i], 16 * (NT // SETS + (i == 0)))

            def rounds(eng, tile):
                for i in range(SETS):
                    tile(i, i, 0, P)
                with eng.Fori(1, NT // SETS) as r:
                    for i in range(SETS):
                        tile(SETS * r + i, i, r, P)
                tile(NT, 0, NT // SETS, NS)

            @block.gpsimd
            def _(pool):
                def tile(t, i, r, n):
                    pool.wait_ge(s_in[i], 32 * r + 32)
                    pool.tensor_tensor(yy[i][0:n, 0, :], yy[i][0:n, 0, :], yy[i][0:n, 1, :], ALU.add).then_inc(s["sum"], 1)

                rounds(pool, tile)

            @block.scalar
            def _(act):
                def tile(t, i, r, n):
                    act.wait_ge(s["x2"], t + 1)
                    act.activation(junk[0:n, :], x1[i][0:n, :], ACT.Square, scale=1.0 / math.sqrt(D), accum_out=ssq[i][0:n, 0:1])
                    act.drain()
                    act.activation(ssq[i][0:n, 0:1], ssq[i][0:n, 0:1], ACT.Sqrt, bias=keep["eps"][0:n, 0:1]).then_inc(s["sq"], 1)

                rounds(act, tile)

            @block.vector
            def _(dve):
                dve.wait_ge(s["f"], 16)

                def tile(t, i, r, n):
                    dve.wait_ge(s["sum"], t + 1)
                    dve.tensor_tensor(yy[i][0:n, 1, :], yy[i][0:n, 0, :], rows[n][0:n, 3, :], ALU.mult)
                    dve.drain()
                    dve.tensor_tensor(x1[i][0:n, :], x1[i][0:n, :], yy[i][0:n, 1, :], ALU.add).then_inc(s["x2"], 1)
                    dve.wait_ge(s["sq"], t + 1)
                    dve.reciprocal(ssq[i][0:n, 1:2], ssq[i][0:n, 0:1])
                    dve.drain()
                    if not (isinstance(t, int) and t < SETS):
                        dve.wait_ge(s_st[i], 16 * r)
                    dve.scalar_tensor_tensor(out=out[i][0:n, :], in0=x1[i][0:n, :], scalar=ssq[i][0:n, 1:2], in1=f_row[0:n, :],
                                             op0=ALU.mult, op1=ALU.mult)
                    dve.drain().then_inc(s["out"], 1)

                rounds(dve, tile)


def build_program(nc, io):
    with ExitStack() as stack:
        k = Kit(nc, stack, clears=False)
        keep = {
            "ident": k.sb("ident", [P, P]), "ones": k.sb("ones", [P, P]), "eps": k.sb("eps", [P, 1]),
            "vecT": k.sb("vecT", [P, NVEC]), "modT": k.sb("modT", [P, 48, 1 + BS]),
            "A1T": k.sb("A1T", [P, KC, 1 + BS]), "coef": k.sb("coef", [P, FC]),
            "w_gate": k.sb("w_gate", [P, 2, FC, P]), "conv0": k.sb("conv0", [P, FC, BS * (CONV - 1)]),
            "h0": k.sb("h0", [P, FC, BS]), "biasP": k.sb("biasP", [P, H]), "nbiasP": k.sb("nbiasP", [P, H]),
        }
        keep["q_blk"] = k.sb("q_blk", [P, BS, H // 2, H * TS])
        keep["kT_new"] = k.sb("kT_new", [P, FC, NS])
        keep["rgT_new"] = k.sb("rgT_new", [P, FC, NS])
        keep["oT_new"] = k.sb("oT_new", [P, FC, NS])
        sems = {"w_in": k.sem("w_in")}
        with ExitStack() as inner:
            keep["w_in"] = Kit(nc, inner, clears=False).sb("w_in", [P, KC, 3 * WA + 2 * WR])
            modulation_phase(nc, io, keep, sems)
            projection_phase(nc, io, keep, sems)
            sample_projection_phase(nc, io, keep, sems)
        keep["n_blocks"] = k.sb("n_blocks", [1, NE], I32)
        keep["rowsP"] = k.sb("rowsP", [P, 4, D])
        keep["rowsS"] = k.sb("rowsS", [NS, 4, D])
        with ExitStack() as inner:
            keep["o_nat"] = Kit(nc, inner, clears=False).sb("o_nat", [P, NT, WA])
            prompt_attention_phase(nc, io, keep)
            sample_attention_phase(nc, io, keep)
            router_phase(nc, io, keep)
        experts_phase(nc, io, keep)
        final_phase(nc, io, keep)


SCRATCH = {"qT_d": ((WA, SEQ), F32), "kT_d": ((WA, SEQ), F32), "rgT_d": ((WR, SEQ), F32),
           "x1_d": ((NTOK, D), F32), "xn_d": ((NTOK, D), F32), "table_d": ((NE * CAP, 4), F32), "y_d": ((2 * NTOK, D), F32)}
INPUTS = ["x_prompt", "x_sample", "cache_k", "cache_v", "state_conv", "state_h", "page_table", "c_prompt", "c_sample",
          "w_ada", "b_ada", "norm_mix", "norm_ffn", "w_in", "sb_bias", "norm_attn", "conv_w", "conv_b", "rg_wa", "rg_ba",
          "rg_wx", "rg_bx", "rg_lambda", "norm_rg", "w_out", "w_group", "b_group", "w_router", "b_router", "w1", "w3",
          "w2", "final_norm"]
OUTPUTS = {"y_prompt": (1, SEQ, D), "y_sample": (BS, TS, D), "k_prompt": (1, 1, SEQ, H, DH), "v_prompt": (1, 1, SEQ, H, DH),
           "conv_prompt": (1, 1, CONV - 1, WR), "h_prompt": (1, 1, WR), "k_sample": (1, BS, TS, H, DH),
           "v_sample": (1, BS, TS, H, DH), "conv_sample": (1, BS, CONV - 1, WR), "h_sample": (1, BS, WR)}


def kernel(**inputs):
    import numpy as _np
    import concourse.bacc as _bacc
    from concourse import mybir as _mybir
    from concourse.bass_utils import run_bass_kernel_spmd as _run

    nc = _bacc.Bacc("TRN2", target_bir_lowering=False, num_devices=1)
    arrays, io = {}, {}
    for name in INPUTS:
        a = _np.ascontiguousarray(inputs[name])
        arrays[f"in_{name}"] = a
        io[name] = nc.dram_tensor(f"in_{name}", a.shape, _mybir.dt.from_np(a.dtype), kind="ExternalInput").ap()
    for name, shape in OUTPUTS.items():
        io[name] = nc.dram_tensor(f"out_{name}", shape, _mybir.dt.float32, kind="ExternalOutput").ap()
    for name, (shape, dt) in SCRATCH.items():
        io[name] = nc.dram_tensor(name, shape, dt, kind="Internal").ap()
    build_program(nc, io)
    r = _run(nc, [arrays], core_ids=[0])
    return tuple(r.results[0][f"out_{name}"] for name in OUTPUTS)
```
